# Optimizing a Trainium2 kernel written in Bass

```python
import math
import jax, jax.numpy as jnp
from jax import lax
import numpy as np

D_MODEL = 2048
BATCH = 1
SEQ = 512
DEPTH = 1

D_SSD = D_MODEL // 2
D_ATT = D_MODEL // 4
D_SC = D_MODEL // 4
D_MIX = D_SSD + D_ATT + D_SC

SSD_HEAD_DIM = 64
SSD_HEADS = D_SSD // SSD_HEAD_DIM
SSD_GROUPS = 2
SSD_HEADS_PER_GROUP = SSD_HEADS // SSD_GROUPS
SSD_STATE = 128
SSD_CONV = 4
SSD_CHUNK = 128
SSD_CONV_DIM = D_SSD + 2 * SSD_GROUPS * SSD_STATE

ATT_HEAD_DIM = 64
ATT_HEADS = D_ATT // ATT_HEAD_DIM
IDX_HEADS = 8
IDX_DIM = 64
TOPK_MAX = 256
Q_BLOCK = 128
REL_BUCKETS = 32
REL_MAX_DIST = 128

SC_GROUPS = 8
SC_CONV = 3

D_FF = 5632
FFN_CONV = 3

NORM_EPS = 1e-6

IN_SIZES = (D_SSD, SSD_CONV_DIM, SSD_HEADS,
            D_ATT, D_ATT, D_ATT,
            IDX_HEADS * IDX_DIM, IDX_DIM, IDX_HEADS,
            D_SC, D_SC, D_SC)
D_IN_PROJ = (D_SSD + SSD_CONV_DIM + SSD_HEADS + 3 * D_ATT
             + IDX_HEADS * IDX_DIM + IDX_DIM + IDX_HEADS + 3 * D_SC)

kernel_name = "hybrid_ssd_dsa_shortconv_block"

def rmsnorm(x, g):
    xf = x.astype(jnp.float32)
    y = xf * lax.rsqrt(jnp.mean(xf * xf, axis=-1, keepdims=True) + NORM_EPS)
    return (y * g.astype(jnp.float32)).astype(x.dtype)

def causal_dwconv(x, w):
    k, c = w.shape
    return lax.conv_general_dilated(
        x, w[:, None, :].astype(x.dtype), window_strides=(1,), padding=[(k - 1, 0)],
        dimension_numbers=('NWC', 'WIO', 'NWC'), feature_group_count=c)

def t5_causal_bucket(dist):
    n = jnp.maximum(dist, 0)
    max_exact = REL_BUCKETS // 2
    large = max_exact + (jnp.log(jnp.maximum(n, max_exact).astype(jnp.float32) / max_exact)
                         / math.log(REL_MAX_DIST / max_exact)
                         * (REL_BUCKETS - max_exact)).astype(jnp.int32)
    large = jnp.minimum(large, REL_BUCKETS - 1)
    return jnp.where(n < max_exact, n, large)

def ssd_chunked_scan(xh, dt, a_head, bm, cm):
    bsz, t = xh.shape[:2]
    nc = t // SSD_CHUNK

    def chunk(a):
        return a.reshape(bsz, nc, SSD_CHUNK, *a.shape[2:])

    x_c = chunk(xh.astype(jnp.float32) * dt[..., None])
    b_c = chunk(bm.astype(jnp.float32))
    c_c = chunk(cm.astype(jnp.float32))
    a_cs = jnp.cumsum(chunk(dt * a_head), axis=2)

    seg = a_cs[:, :, :, None] - a_cs[:, :, None, :]
    tril = jnp.tril(jnp.ones((SSD_CHUNK, SSD_CHUNK), dtype=bool))[:, :, None, None]
    lmat = jnp.exp(jnp.where(tril, seg, -jnp.inf))
    cb = jnp.einsum('bclgn,bcsgn->bclsg', c_c, b_c)
    y_diag = jnp.einsum('bclsg,bclsgr,bcsgrp->bclgrp', cb, lmat, x_c)

    decay_to_end = jnp.exp(a_cs[:, :, -1:] - a_cs)
    chunk_states = jnp.einsum('bclgn,bclgr,bclgrp->bcgrpn', b_c, decay_to_end, x_c)
    chunk_decay = jnp.exp(a_cs[:, :, -1])

    def step(h, inp):
        s_c, d_c = inp
        return h * d_c[..., None, None] + s_c, h

    h0 = jnp.zeros((bsz, SSD_GROUPS, SSD_HEADS_PER_GROUP, SSD_HEAD_DIM, SSD_STATE), jnp.float32)
    _, h_prev = lax.scan(step, h0, (jnp.moveaxis(chunk_states, 1, 0), jnp.moveaxis(chunk_decay, 1, 0)))
    h_prev = jnp.moveaxis(h_prev, 0, 1)
    y_off = jnp.einsum('bclgn,bcgrpn,bclgr->bclgrp', c_c, h_prev, jnp.exp(a_cs))
    return (y_diag + y_off).reshape(bsz, t, SSD_GROUPS, SSD_HEADS_PER_GROUP, SSD_HEAD_DIM)

def ssd_mixer(z, xbc, dt_raw, conv_w, conv_b, dt_bias, a_log, d_skip, norm_g):
    bsz, t, _ = z.shape
    xbc = jax.nn.silu(causal_dwconv(xbc, conv_w) + conv_b.astype(xbc.dtype))
    xs, bm, cm = jnp.split(xbc, [D_SSD, D_SSD + SSD_GROUPS * SSD_STATE], axis=-1)
    xh = xs.reshape(bsz, t, SSD_GROUPS, SSD_HEADS_PER_GROUP, SSD_HEAD_DIM)
    bm = bm.reshape(bsz, t, SSD_GROUPS, SSD_STATE)
    cm = cm.reshape(bsz, t, SSD_GROUPS, SSD_STATE)
    dt = jax.nn.softplus(dt_raw.astype(jnp.float32) + dt_bias.astype(jnp.float32))
    dt = dt.reshape(bsz, t, SSD_GROUPS, SSD_HEADS_PER_GROUP)
    a_head = -jnp.exp(a_log.astype(jnp.float32)).reshape(SSD_GROUPS, SSD_HEADS_PER_GROUP)
    y = ssd_chunked_scan(xh, dt, a_head, bm, cm)
    y = y + xh.astype(jnp.float32) * d_skip.astype(jnp.float32).reshape(SSD_GROUPS, SSD_HEADS_PER_GROUP, 1)
    y = y.reshape(bsz, t, D_SSD) * jax.nn.silu(z.astype(jnp.float32))
    y = rmsnorm(y.reshape(bsz, t, SSD_GROUPS, D_SSD // SSD_GROUPS),
                norm_g.reshape(SSD_GROUPS, D_SSD // SSD_GROUPS))
    return y.reshape(bsz, t, D_SSD).astype(z.dtype)

def dsa_mixer(q, k, v, q_idx, k_idx, w_idx, q_norm, k_norm, rel_bias):
    bsz, t, _ = q.shape
    q = rmsnorm(q.reshape(bsz, t, ATT_HEADS, ATT_HEAD_DIM), q_norm)
    k = rmsnorm(k.reshape(bsz, t, ATT_HEADS, ATT_HEAD_DIM), k_norm)
    v = v.reshape(bsz, t, ATT_HEADS, ATT_HEAD_DIM)
    qi = q_idx.reshape(bsz, t, IDX_HEADS, IDX_DIM)
    top_k = min(TOPK_MAX, t // 4)
    nb = t // Q_BLOCK
    scale = ATT_HEAD_DIM ** -0.5
    key_pos = jnp.arange(t, dtype=jnp.int32)
    gather = jax.vmap(lambda a, i: a[i])

    def to_blocks(a):
        return jnp.moveaxis(a.reshape(bsz, nb, Q_BLOCK, *a.shape[2:]), 1, 0)

    def block(args):
        start, qb, qib, wb = args
        qpos = start + jnp.arange(Q_BLOCK, dtype=jnp.int32)
        rel = jax.nn.relu(jnp.einsum('bqhd,bsd->bqsh', qib, k_idx).astype(jnp.float32))
        score = jnp.einsum('bqsh,bqh->bqs', rel, wb.astype(jnp.float32))
        causal = key_pos[None, :] <= qpos[:, None]
        score = jnp.where(causal[None], score, -jnp.inf)
        _, sel = lax.top_k(score, top_k)
        k_sel = gather(k, sel)
        v_sel = gather(v, sel)
        dist = qpos[None, :, None] - sel
        valid = dist >= 0
        bias = rel_bias[t5_causal_bucket(dist)].astype(jnp.float32)
        logits = (jnp.einsum('bqhd,bqkhd->bhqk', qb, k_sel).astype(jnp.float32) * scale
                  + jnp.moveaxis(bias, -1, 1))
        logits = jnp.where(valid[:, None], logits, -jnp.inf)
        p = jax.nn.softmax(logits, axis=-1).astype(v.dtype)
        return jnp.einsum('bhqk,bqkhd->bqhd', p, v_sel)

    starts = jnp.arange(nb, dtype=jnp.int32) * Q_BLOCK
    out = lax.map(block, (starts, to_blocks(q), to_blocks(qi), to_blocks(w_idx)))
    return jnp.moveaxis(out, 0, 1).reshape(bsz, t, D_ATT)

def setup_inputs(seed: int = 0) -> dict:
    key = jax.random.key(seed)
    ks = jax.random.split(key, 20)

    def nrm(k, shape, s):
        return jax.random.normal(k, shape, jnp.float32) * s

    x = nrm(ks[0], (BATCH, SEQ, D_MODEL), 1.0)
    norm_mix = 1.0 + nrm(ks[1], (DEPTH, D_MODEL), 0.02)
    w_in = nrm(ks[2], (DEPTH, D_MODEL, D_IN_PROJ), D_MODEL ** -0.5)
    ssd_conv_w = nrm(ks[3], (DEPTH, SSD_CONV, SSD_CONV_DIM), SSD_CONV ** -0.5)
    ssd_conv_b = nrm(ks[4], (DEPTH, SSD_CONV_DIM), 0.02)
    dt0 = jnp.exp(jax.random.uniform(ks[5], (DEPTH, SSD_HEADS), jnp.float32,
                                     minval=math.log(1e-3), maxval=math.log(1e-1)))
    ssd_dt_bias = dt0 + jnp.log(-jnp.expm1(-dt0))
    ssd_a_log = jnp.log(jax.random.uniform(ks[6], (DEPTH, SSD_HEADS), jnp.float32, minval=1.0, maxval=16.0))
    ssd_d = 1.0 + nrm(ks[7], (DEPTH, SSD_HEADS), 0.1)
    ssd_norm = 1.0 + nrm(ks[8], (DEPTH, D_SSD), 0.02)
    att_q_norm = 1.0 + nrm(ks[9], (DEPTH, ATT_HEAD_DIM), 0.02)
    att_k_norm = 1.0 + nrm(ks[10], (DEPTH, ATT_HEAD_DIM), 0.02)
    rel_bias = nrm(ks[11], (REL_BUCKETS, ATT_HEADS), 0.5)
    sc_conv_w = nrm(ks[12], (DEPTH, SC_CONV, D_SC), SC_CONV ** -0.5)
    w_out = nrm(ks[13], (DEPTH, D_MIX, D_MODEL), D_MIX ** -0.5)
    norm_ffn = 1.0 + nrm(ks[14], (DEPTH, D_MODEL), 0.02)
    ffn_w_gate = nrm(ks[15], (DEPTH, D_MODEL, D_FF), D_MODEL ** -0.5)
    ffn_w_up = nrm(ks[16], (DEPTH, D_MODEL, D_FF), D_MODEL ** -0.5)
    ffn_conv_w = nrm(ks[17], (DEPTH, FFN_CONV, D_FF), FFN_CONV ** -0.5)
    ffn_w_down = nrm(ks[18], (DEPTH, D_FF, D_MODEL), D_FF ** -0.5)
    return {"x": x, "norm_mix": norm_mix, "w_in": w_in,
            "ssd_conv_w": ssd_conv_w, "ssd_conv_b": ssd_conv_b, "ssd_dt_bias": ssd_dt_bias,
            "ssd_a_log": ssd_a_log, "ssd_d": ssd_d, "ssd_norm": ssd_norm,
            "att_q_norm": att_q_norm, "att_k_norm": att_k_norm, "rel_bias": rel_bias,
            "sc_conv_w": sc_conv_w, "w_out": w_out, "norm_ffn": norm_ffn,
            "ffn_w_gate": ffn_w_gate, "ffn_w_up": ffn_w_up, "ffn_conv_w": ffn_conv_w,
            "ffn_w_down": ffn_w_down}

def reference(x, norm_mix, w_in, ssd_conv_w, ssd_conv_b, ssd_dt_bias, ssd_a_log, ssd_d, ssd_norm,
              att_q_norm, att_k_norm, rel_bias, sc_conv_w, w_out, norm_ffn,
              ffn_w_gate, ffn_w_up, ffn_conv_w, ffn_w_down):
    split_points = np.cumsum(np.array(IN_SIZES))[:-1].tolist()
    for l in range(DEPTH):
        h = rmsnorm(x, norm_mix[l])
        proj = h @ w_in[l]
        (z, xbc, dt_raw, q, k, v, q_idx, k_idx, w_idx,
         sc_b, sc_c, sc_h) = jnp.split(proj, split_points, axis=-1)
        y_ssd = ssd_mixer(z, xbc, dt_raw, ssd_conv_w[l], ssd_conv_b[l], ssd_dt_bias[l],
                          ssd_a_log[l], ssd_d[l], ssd_norm[l])
        y_att = dsa_mixer(q, k, v, q_idx, k_idx, w_idx, att_q_norm[l], att_k_norm[l], rel_bias)
        y_sc = sc_b * causal_dwconv(sc_c * sc_h, sc_conv_w[l])
        x = x + jnp.concatenate([y_ssd, y_att, y_sc], axis=-1) @ w_out[l]
        h2 = rmsnorm(x, norm_ffn[l])
        g = causal_dwconv(h2 @ ffn_w_gate[l], ffn_conv_w[l])
        x = x + (jax.nn.silu(g) * (h2 @ ffn_w_up[l])) @ ffn_w_down[l]
    return x


_drawn_inputs = setup_inputs


def setup_inputs(seed=0):
    import zlib

    import numpy as np

    out = dict(_drawn_inputs(seed))
    spreads = {}
    factors = {'ssd_conv_b': 3.632,
     'ssd_norm': 5.276,
     'att_q_norm': 8.0,
     'att_k_norm': 8.0,
     'norm_ffn': 4.648,
     'rel_bias': 7.434}
    for name, (base, spread) in spreads.items():
        noise = np.random.default_rng([zlib.crc32(name.encode()), seed]).standard_normal(out[name].shape)
        drawn = base * np.exp(spread * noise) if base else spread * noise
        out[name] = __import__('jax').numpy.asarray(drawn.astype(out[name].dtype))
    for name, factor in factors.items():
        out[name] = (out[name] * factor).astype(out[name].dtype)
    return out
```

```python
from contextlib import ExitStack

import numpy as np
import concourse.bass as bass
from concourse import mybir


P = 128
T = 512
D = 2048
KT = D // P
NCH = T // P
D_FF = 5632
FT = D_FF // P
FCH = 4
FPC = FT // FCH
HEADS = 8
SSD_HEADS = 16
TOPK = 128
BUCKETS = 32

D_SSD, D_ATT, D_SC = 1024, 512, 512
OFF_Z = 0
OFF_XS = OFF_Z + D_SSD
OFF_B = OFF_XS + D_SSD
OFF_C = OFF_B + 256
OFF_DT = OFF_C + 256
OFF_Q = OFF_DT + SSD_HEADS
OFF_K = OFF_Q + D_ATT
OFF_V = OFF_K + D_ATT
OFF_QI = OFF_V + D_ATT
OFF_KI = OFF_QI + 512
OFF_WI = OFF_KI + 64
OFF_SCB = OFF_WI + 8
OFF_SCC = OFF_SCB + D_SC
OFF_SCH = OFF_SCC + D_SC

M_KI, M_DT, M_WI = 0, 64, 96


def proj_tiles():
    tiles = [("misc", 0, None)]
    tiles += [("qi", j, OFF_QI + P * j) for j in range(4)]
    tiles += [("q", j, OFF_Q + P * j) for j in range(4)]
    tiles += [("k", j, OFF_K + P * j) for j in range(4)]
    tiles += [("v", j, OFF_V + P * j) for j in range(4)]
    for s in range(2):
        tiles += [("scb", s, OFF_SCB + P * s), ("scc", s, OFF_SCC + P * s), ("sch", s, OFF_SCH + P * s)]
    tiles += [("conv", j, OFF_B + P * j) for j in range(4)]
    for j in range(8):
        tiles += [("z", j, OFF_Z + P * j), ("conv", 4 + j, OFF_XS + P * j)]
    for s in range(2, 4):
        tiles += [("scb", s, OFF_SCB + P * s), ("scc", s, OFF_SCC + P * s), ("sch", s, OFF_SCH + P * s)]
    return tiles


TILES = proj_tiles()
NPROJ = len(TILES)
TILE_OF = {(kind, j): t for t, (kind, j, _) in enumerate(TILES)}

QN_OUT = 4 * NPROJ
QN_FFN = QN_OUT + 4 * KT
QN_CHUNK = 8 * FPC + 4 * KT
TN_OUT = NPROJ
TN_FFN = NPROJ + KT
TN_CHUNK = 2 * FPC + KT
NRAW, NW = 4, 8
DOWN_K = [(0, 3), (3, 3), (6, 3), (9, 2)]

PC_NAMES = [("gmix", 16), ("gffn", 16), ("cw", 48), ("cb", 12), ("scw", 12), ("fcw", 132), ("dskip", 8),
            ("gssd", 8), ("gq", 1), ("gk", 1), ("dtb", 16), ("alog", 16), ("eps", 1)]
PC = {}
_n = 0
for _name, _w in PC_NAMES:
    PC[_name] = _n
    _n += _w
NPC = _n

CM_NAMES = ["ident", "triu", "after", "causal", "ones", "halves"]
NEG = -1.0e30
TAKEN = -3.0e38
EPS = 1e-6

IDX_AT = 4 * 5 + 1
TOPK_AT = 4 * 8 + 2
ATT_AT = 4 * 17
N_IDX = 3 * HEADS
N_ROUND = 3 * (TOPK // 8)
N_ATT = HEADS * NCH
SPLIT_AT = 4 * 46

LOG1P = [1.0 / (2 * i + 1) for i in range(9)]


def hybrid_block(nc, xT, w_in, w_out, w_gu, w_dn, params, relb, cmats, onehot, bias_rows, acs_rows, out):
    F32, F32R = mybir.dt.float32, mybir.dt.float32r
    ALU = mybir.AluOpType
    ACT = mybir.ActivationFunctionType

    with ExitStack() as ctx:
        def sb(name, shape, dt=F32):
            return ctx.enter_context(nc.sbuf_tensor(name, shape, dt))

        def sem(name):
            return ctx.enter_context(nc.semaphore(name))

        resid = sb("resid", [P, KT, T])
        hhi = sb("hhi", [P, KT, T], F32R)
        hlo = sb("hlo", [P, KT, T], F32R)
        raw = sb("raw", [P, NRAW, T])
        whi = sb("whi", [P, NW, T], F32R)
        wlo = sb("wlo", [P, NW, T], F32R)
        cm = sb("cm", [P, len(CM_NAMES), P])
        pc = sb("pc", [P, NPC])
        sqsum = sb("sqsum", [P, T])
        with ExitStack() as r:
            work = r.enter_context(nc.sbuf_tensor("work", [P, 32 * T], F32))
        with ExitStack() as r:
            yhi = r.enter_context(nc.sbuf_tensor("yhi", [P, KT, T], F32R))
            ylo = r.enter_context(nc.sbuf_tensor("ylo", [P, KT, T], F32R))
        with ExitStack() as r:
            ahi = r.enter_context(nc.sbuf_tensor("ahi", [P, FPC, T], F32R))
            alo = r.enter_context(nc.sbuf_tensor("alo", [P, FPC, T], F32R))
            rstd2 = r.enter_context(nc.sbuf_tensor("rstd2", [P, T], F32))
            ntmp2 = r.enter_context(nc.sbuf_tensor("ntmp2", [P, T], F32))
            gpad = r.enter_context(nc.sbuf_tensor("gpad", [P, T + 2], F32))
            gconv = r.enter_context(nc.sbuf_tensor("gconv", [P, T], F32))
            gsilu = r.enter_context(nc.sbuf_tensor("gsilu", [P, T], F32))
            upv = r.enter_context(nc.sbuf_tensor("upv", [P, T], F32))
            act = r.enter_context(nc.sbuf_tensor("act", [P, T], F32))

        def C(name):
            return cm[:, CM_NAMES.index(name), :]

        def par(name, j=0, n=1):
            return pc[:, PC[name] + j:PC[name] + j + n]

        def wk(at, n):
            return work[:, at:at + n]

        qi = wk(0, 2048).rearrange("p (j t) -> p j t", j=4)
        relu = wk(2048, 1024).rearrange("p (j t) -> p j t", j=2)
        misc = wk(3072, 512)
        ki_hi = wk(3584, 512)
        vT = wk(3072, 1024).rearrange("p (j t) -> p j t", j=2)
        nsq = wk(4096, 1024).rearrange("p (j t) -> p j t", j=2)
        pT = wk(4096, 1024).rearrange("p (j t) -> p j t", j=2)
        nrs = wk(5248, 512)
        ntmp = wk(5760, 512)
        qkT = wk(6272, 4096).rearrange("p (j t) -> p j t", j=8)
        vtok = wk(10368, 2048).rearrange("p (c d) -> p c d", c=4)
        score_at = {1: 12416, 2: 12416 + 256, 3: 12416 + 640}
        score = {b: wk(score_at[b], P * (b + 1)) for b in (1, 2, 3)}
        rrow = work[0:HEADS, 13568:13568 + 384]
        small = 13952
        dt = wk(small, 64).rearrange("p (c h) -> p c h", c=4)
        dta = wk(small + 64, 64)
        widx = wk(small + 128, 32).rearrange("p (c h) -> p c h", c=4)
        far = wk(small + 160, 8)
        top8 = wk(small + 168, 8)
        rmax = wk(small + 176, 4)
        nmax = wk(small + 180, 4)
        rsum = wk(small + 184, 4)
        rinv = wk(small + 188, 4)
        acs = wk(small + 192, 64)
        to_end = wk(small + 256, 64)
        total = wk(small + 320, 64)
        ealog = wk(8084, 16)
        acs_row = resid[0:4 * SSD_HEADS, 7, 0:P]
        oneh_t = work[0:BUCKETS, 7168:7680]
        relt = work[0:BUCKETS, 7680:7688]
        sp = [wk(7700 + 64 * i, 64).rearrange("p (c h) -> p c h", c=4) for i in range(6)]
        scb = wk(14336, 512)
        scm = wk(14848, 514)
        scu = wk(15362, 512)
        cpad = wk(0, 515)
        cacc = wk(520, 512)
        bT = wk(1032, 1024).rearrange("p (g t) -> p g t", g=2)
        cT = wk(2056, 1024).rearrange("p (g t) -> p g t", g=2)
        btok = wk(3080, 1024).rearrange("p (g c n) -> p g c n", g=2, c=4)
        cbt = wk(4104, 1024).rearrange("p (g c l) -> p g c l", g=2, c=4)
        zs = wk(6272, 1024).rearrange("p (j t) -> p j t", j=2)
        xsT = wk(7296, 512)
        rows = wk(7808, 1024).rearrange("p (h c l) -> p h c l", h=2, c=4)
        gmat = wk(8832, 1024).rearrange("p (h c l) -> p h c l", h=2, c=4)
        ce = wk(9856, 768).rearrange("p (h c l) -> p h c l", h=2, c=3)
        xdt = wk(10624, 512).rearrange("p (c h d) -> p c h d", c=4, h=2)
        xdd = wk(11136, 384).rearrange("p (c h d) -> p c h d", c=3, h=2)
        hst = wk(11520, 384).rearrange("p (c h d) -> p c h d", c=3, h=2)
        gsum = wk(11904, 512)
        gtmp = wk(12416, 512)
        btile = resid[:, 0:4, :].rearrange("p a b -> p (a b)").rearrange("p (h k) -> p h k", h=HEADS)
        logit = resid[:, 4:8, :]

        ps = ctx.enter_context(nc.psum_tensor("ps", [P, 8, T], F32))

        def bank(i):
            return ps[:, i, :]

        par_loaded, const_loaded = sem("par_loaded"), sem("const_loaded")
        x_loaded = [sem(f"x_loaded{i}") for i in range(8)]
        raw_loaded = [sem(f"raw_loaded{i}") for i in range(NRAW)]
        hi_ready, lo_ready, w_used = sem("hi_ready"), sem("lo_ready"), sem("w_used")
        acc_read = [sem("acc_read0"), sem("acc_read1")]
        x_sq, x_acc, x_r0 = sem("x_sq"), sem("x_acc"), sem("x_r0")
        h_hi, h_lo, x_sum = sem("h_hi"), sem("h_lo"), sem("x_sum")
        vec, act_step = sem("vec"), sem("act_step")
        rows_ready, rows_copied, rows_stored, btile_loaded = sem("rows_ready"), sem("rows_copied"), sem("rows_stored"), sem("btile_loaded")
        ki_dup, misc_tok, misc_used = sem("ki_dup"), sem("misc_tok"), sem("misc_used")
        sp_in, sp_exp, dt_ready = sem("sp_in"), sem("sp_exp"), sem("dt_ready")
        acs_sum, acs_copied, acs_diff, acs_exp = sem("acs_sum"), sem("acs_copied"), sem("acs_diff"), sem("acs_exp")
        acs_stored, rows_loaded = sem("acs_stored"), sem("rows_loaded")
        z_silu = sem("z_silu")
        idx_s, idx_relu, idx_acc = sem("idx_s"), sem("idx_relu"), sem("idx_acc")
        mask_ready = sem("mask_ready")
        nq_sq, nq_sum, nq_r0, nq_done = sem("nq_sq"), sem("nq_sum"), sem("nq_r0"), sem("nq_done")
        v_tr, v_tok = sem("v_tr"), sem("v_tok")
        att_s, att_log, att_max, att_exp = sem("att_s"), sem("att_log"), sem("att_max"), sem("att_exp")
        att_p, att_t, att_pt, att_pv, att_out = sem("att_p"), sem("att_t"), sem("att_pt"), sem("att_pv"), sem("att_out")
        sc_m, sc_done = sem("sc_m"), sem("sc_done")
        conv_done, conv_silu = sem("conv_done"), sem("conv_silu")
        bc_prep, bc_done = sem("bc_prep"), sem("bc_done")
        seg_ready, lt_ready, g_ready = sem("seg_ready"), sem("lt_ready"), sem("g_ready")
        xs_tr, xdt_ready, st_ready, hst_ready = sem("xs_tr"), sem("xdt_ready"), sem("st_ready"), sem("hst_ready")
        y_ready, y_done, gn_sum, gn_r0, gn_done = sem("y_ready"), sem("y_done"), sem("gn_sum"), sem("gn_r0"), sem("gn_done")
        y_hi, y_lo = sem("y_hi"), sem("y_lo")
        x2_sq, x2_sum, h2_hi, h2_lo = sem("x2_sq"), sem("x2_sum"), sem("h2_hi"), sem("h2_lo")
        r2_sum, r2_r0, r2_done = sem("r2_sum"), sem("r2_r0"), sem("r2_done")
        f_conv, f_silu, f_act, a_hi, a_lo = sem("f_conv"), sem("f_silu"), sem("f_act"), sem("a_hi"), sem("a_lo")
        out_stored = sem("out_stored")

        block = ctx.enter_context(nc.Block())

        class Chain:

            def __init__(self, eng, s):
                self.eng, self.s, self.n, self.base = eng, s, 0, 0

            def link(self, ins):
                self.n += 1
                ins.then_inc(self.s, 1)
                self.eng.wait_ge(self.s, self.base + self.n)

        def wait_tile(eng, t):
            eng.wait_ge(w_used, 4 * (t + 1))

        def wait_read(eng, t):
            eng.wait_ge(acc_read[t % 2], t // 2 + 1)

        @block.sync
        def _(sp_):
            def load(slot, n, src, width):
                sp_.wait_ge(lo_ready, n - NRAW + 1)
                sp_.dma_start(raw[:, slot % NRAW, 0:width], src).then_inc(raw_loaded[slot % NRAW], 16)

            for q in range(NRAW):
                sp_.dma_start(raw[:, q, :], w_in[0, :, q * T:(q + 1) * T]).then_inc(raw_loaded[q], 16)
            with sp_.Fori(1, NPROJ) as t:
                for q in range(4):
                    load(q, 4 * t + q, w_in[bass.ds(t, 1), :, q * T:(q + 1) * T].rearrange("a p n -> (a p) n"), T)
            with sp_.Fori(0, KT) as t:
                for q in range(4):
                    load(q, 4 * t + (QN_OUT + q), w_out[bass.ds(t, 1), :, q * T:(q + 1) * T].rearrange("a p n -> (a p) n"), T)
            with sp_.Fori(0, FCH) as c:
                with sp_.Fori(0, 2 * FPC) as f:
                    for q in range(4):
                        load(q, QN_CHUNK * c + 4 * f + (QN_FFN + q),
                             w_gu[bass.ds(2 * FPC * c + f, 1), :, q * T:(q + 1) * T].rearrange("a p n -> (a p) n"), T)
                with sp_.Fori(0, KT) as d:
                    for q, (k0, kn) in enumerate(DOWN_K):
                        load(q, QN_CHUNK * c + 4 * d + (QN_FFN + 8 * FPC + q),
                             w_dn[bass.ds(KT * c + d, 1), :, k0 * P:(k0 + kn) * P].rearrange("a p n -> (a p) n"), kn * P)

        @block.gpsimd
        def _(pool):
            def low(slot, n, width):
                pool.wait_ge(hi_ready, n + 1)
                nc.gpsimd.tensor_tensor(wlo[:, slot % NW, 0:width], raw[:, slot % NRAW, 0:width],
                                        whi[:, slot % NW, 0:width].bitcast(F32), ALU.subtract).then_inc(lo_ready, 1)

            with pool.Fori(0, (QN_OUT - 4) // 8) as i:
                for q in range(8):
                    low(q, 8 * i + q, T)
            for q in range(QN_OUT - 4, QN_OUT):
                low(q, q, T)
            with pool.Fori(0, KT // 2) as i:
                for q in range(8):
                    low(QN_OUT + q, 8 * i + (QN_OUT + q), T)
            with pool.Fori(0, FCH) as c:
                with pool.Fori(0, FPC) as f:
                    for q in range(8):
                        low(QN_FFN + q, QN_CHUNK * c + 8 * f + (QN_FFN + q), T)
                with pool.Fori(0, KT // 2) as d:
                    for q in range(8):
                        low(QN_FFN + q, QN_CHUNK * c + 8 * d + (QN_FFN + 8 * FPC + q), DOWN_K[q % 4][1] * P)

        @block.tensor
        def _(pe):
            def quarter(slot, n, parity, src_hi, src_lo, ks, first, last, before=None):
                pe.wait_ge(lo_ready, n + 1)
                for i, k in enumerate(ks):
                    if before is not None:
                        before(k)
                    w = slice(i * P, (i + 1) * P)
                    s = slot % NW
                    nc.tensor.matmul(bank(parity), whi[:, s, w], src_hi[:, k, :], start=first and i == 0, stop=False)
                    nc.tensor.matmul(bank(parity), wlo[:, s, w], src_hi[:, k, :], start=False, stop=False)
                    ins = nc.tensor.matmul(bank(parity), whi[:, s, w], src_lo[:, k, :], start=False,
                                           stop=last and i == len(ks) - 1)
                ins.then_inc(w_used, 1)

            def side(t, q):
                a = 4 * t + q
                kind, j, _ = TILES[t - 1] if 0 < t <= NPROJ else ("", 0, 0)
                if (t, q) == (1, 0):
                    pe.wait_ge(const_loaded, 16 * 3)
                    nc.tensor.matmul(ps[0:HEADS, 4, 0:384], relt, oneh_t[:, 0:384], start=True, stop=True)
                    nc.tensor.matmul(ps[:, 5, 0:HEADS], oneh_t[:, 384:512], relt, start=True, stop=True).then_inc(rows_ready, 1)
                if (t, q) == (1, 3):
                    pe.wait_ge(x_acc, KT - 1)
                    nc.tensor.matmul(bank(2), C("ones"), sqsum[:, :], start=True, stop=True).then_inc(x_sum, 1)
                if (t, q) == (2, 1):
                    wait_read(pe, 0)
                    for c in range(NCH):
                        ins = nc.tensor.transpose(ps[:, 3, c * P:(c + 1) * P], misc[:, c * P:(c + 1) * P], C("ident"))
                    ins.then_inc(misc_tok, 1)
                if (t, q) == (4, 1):
                    pe.wait_ge(dt_ready, 1)
                    pe.wait_ge(misc_used, 1)
                    nc.tensor.matmul(ps[0:64, 3, 0:P], dta, C("triu"), start=True, stop=True)
                    nc.tensor.matmul(ps[:, 3, P:P + 64], C("triu"), dta, start=True, stop=True)
                    nc.tensor.matmul(ps[:, 3, P + 64:P + 128], C("ones"), dta, start=True, stop=True).then_inc(acs_sum, 1)
                if kind in ("q", "k") and q == 1:
                    m = j + (4 if kind == "k" else 0)
                    pe.wait_ge(nq_sq, m + 1)
                    if m >= 2:
                        pe.wait_ge(nq_done, m - 1)
                    nc.tensor.matmul(bank(4 + m % 2), C("halves"), nsq[:, m % 2, :], start=True, stop=True).then_inc(nq_sum, 1)
                if kind == "v" and q == 1:
                    wait_read(pe, t - 1)
                    if j >= 2:
                        pe.wait_ge(v_tok, j - 1)
                    for c in range(NCH):
                        ins = nc.tensor.transpose(ps[:, 6 + j % 2, c * P:(c + 1) * P], vT[:, j % 2, c * P:(c + 1) * P], C("ident"))
                    ins.then_inc(v_tr, 1)
                if IDX_AT <= a < IDX_AT + N_IDX // 2:
                    for e in (2 * (a - IDX_AT), 2 * (a - IDX_AT) + 1):
                        b, h = 1 + e // HEADS, e % HEADS
                        if e == 0:
                            wait_read(pe, TILE_OF["qi", 3])
                            wait_read(pe, TILE_OF["qi", 2])
                            pe.wait_ge(ki_dup, 16)
                            pe.wait_ge(acs_copied, 2)
                            pe.wait_ge(acs_diff, 1)
                        if e >= 2:
                            pe.wait_ge(idx_relu, e - 1)
                        rows = slice(64 * (h % 2), 64 * (h % 2) + 64)
                        key = misc if h % 2 == 0 else ki_hi
                        nc.tensor.matmul(ps[:, 2 + e % 2, 0:P * (b + 1)], qi[rows, h // 2, b * P:(b + 1) * P],
                                         key[rows, 0:P * (b + 1)], start=True, stop=True).then_inc(idx_s, 1)
                if ATT_AT <= a < ATT_AT + N_ATT + 3:
                    u = a - ATT_AT - 2
                    if 0 <= u < N_ATT:
                        b = u % NCH
                        pe.wait_ge(att_p, u + 1)
                        if u >= 2:
                            pe.wait_ge(att_pt, u - 1)
                        for kb in range(b + 1):
                            ins = nc.tensor.transpose(ps[:, 4 + u % 2, kb * P:(kb + 1) * P],
                                                      logit[:, u % 4, kb * P:(kb + 1) * P], C("ident"))
                        ins.then_inc(att_t, 1)
                    u = a - ATT_AT - 3
                    if 0 <= u < N_ATT:
                        h, b = u // NCH, u % NCH
                        pe.wait_ge(att_pt, u + 1)
                        if u == 0:
                            pe.wait_ge(v_tok, 4)
                        if h >= 4 and h % 2 == 0 and b == 0:
                            pe.wait_ge(att_out, h // 2 - 1)
                        for kb in range(b + 1):
                            ins = nc.tensor.matmul(ps[64 * (h % 2):64 * (h % 2) + 64, 6 + (h // 2) % 2, b * P:(b + 1) * P],
                                                   vtok[:, kb, h * 64:(h + 1) * 64], pT[:, u % 2, kb * P:(kb + 1) * P],
                                                   start=kb == 0, stop=kb == b)
                        ins.then_inc(att_pv, 1)
                    u = a - ATT_AT
                    if u < N_ATT:
                        h, b = u // NCH, u % NCH
                        if u == 0:
                            pe.wait_ge(nq_done, 8)
                        if u >= 2:
                            pe.wait_ge(att_log, u - 1)
                        rows = slice(64 * (h % 2), 64 * (h % 2) + 64)
                        nc.tensor.matmul(ps[:, 2 + u % 2, 0:P * (b + 1)], qkT[rows, h // 2, b * P:(b + 1) * P],
                                         qkT[rows, 4 + h // 2, 0:P * (b + 1)], start=True, stop=True).then_inc(att_s, 1)
                if (t, q) == (27, 3):
                    pe.wait_ge(conv_silu, 4)
                    pe.wait_ge(att_out, 4)
                    for g in range(2):
                        for c in range(NCH):
                            nc.tensor.transpose(ps[:, 6 + g, c * P:(c + 1) * P], bT[:, g, c * P:(c + 1) * P], C("ident"))
                        for c in range(NCH):
                            ins = nc.tensor.matmul(ps[:, 2 + g, c * P:(c + 1) * P], bT[:, g, c * P:(c + 1) * P],
                                                   cT[:, g, c * P:(c + 1) * P], start=True, stop=True)
                    ins.then_inc(bc_prep, 1)
                if t >= 28:
                    if (t - 29) % 2 == 0 and 0 <= (t - 29) // 2 < 8 and q == 2:
                        j2 = (t - 29) // 2
                        pe.wait_ge(conv_silu, 5 + j2)
                        pe.wait_ge(hst_ready, j2) if j2 else pe.wait_ge(bc_done, 1)
                        for c in range(NCH):
                            ins = nc.tensor.transpose(ps[:, 6, c * P:(c + 1) * P], xsT[:, c * P:(c + 1) * P], C("ident"))
                        ins.then_inc(xs_tr, 1)
                    if (t - 29) % 2 == 0 and 0 <= (t - 29) // 2 < 8 and q == 3:
                        j2 = (t - 29) // 2
                        pe.wait_ge(xdt_ready, j2 + 1)
                        for c in range(NCH - 1):
                            ins = nc.tensor.matmul(ps[:, 6, c * P:(c + 1) * P], btok[:, j2 // 4, c, :],
                                                   xdd[:, c, :, :].rearrange("p h d -> p (h d)"), start=True, stop=True)
                        ins.then_inc(st_ready, 1)
                    if (t - 30) % 2 == 0 and 0 <= (t - 30) // 2 < 8 and q == 0:
                        j2 = (t - 30) // 2
                        pe.wait_ge(hst_ready, j2 + 1)
                        pe.wait_ge(g_ready, j2 + 1)
                        if j2 >= 1:
                            pe.wait_ge(y_done, j2)
                        if j2 == 4:
                            pe.wait_ge(gn_done, 1)
                        for hh in range(2):
                            for c in range(NCH):
                                o = ps[64 * hh:64 * hh + 64, 7, c * P:(c + 1) * P]
                                ins = nc.tensor.matmul(o, xdt[:, c, hh, :], gmat[:, hh, c, :], start=True, stop=c == 0)
                                if c:
                                    ins = nc.tensor.matmul(o, hst[:, c - 1, hh, :], ce[:, hh, c - 1, :], start=False, stop=True)
                        ins.then_inc(y_ready, 1)
                    if (t, q) in ((36, 2), (44, 2)):
                        pe.wait_ge(y_done, 4 if t == 36 else 8)
                        nc.tensor.matmul(bank(7), C("ones"), gsum, start=True, stop=True).then_inc(gn_sum, 1)

            for t in range(NPROJ):
                for q in range(4):
                    side(t, q)
                    if q == 0 and t >= 2:
                        wait_read(pe, t - 2)
                    quarter(4 * t + q, 4 * t + q, t % 2, hhi, hlo, range(4 * q, 4 * q + 4), q == 0, q == 3,
                            (lambda k: pe.wait_ge(h_lo, k + 1)) if t == 0 else None)

            for c in range(2):
                wait_read(pe, TN_OUT + c - 2)
                for q in range(4):
                    n = QN_OUT + 4 * c + q
                    quarter(n, n, (TN_OUT + c) % 2, yhi, ylo, range(4 * q, 4 * q + 4), q == 0, q == 3,
                            (lambda k: pe.wait_ge(y_lo, k + 1)) if c == 0 else None)
            with pe.Fori(1, KT // 2) as i:
                for c in range(2):
                    pe.wait_ge(acc_read[(TN_OUT + c) % 2], i + (TN_OUT + c - 2) // 2 + 1)
                    for q in range(4):
                        quarter(QN_OUT + 4 * c + q, 8 * i + (QN_OUT + 4 * c + q), (TN_OUT + c) % 2, yhi, ylo,
                                range(4 * q, 4 * q + 4), q == 0, q == 3)

            pe.wait_ge(x2_sum, KT + 1)
            nc.tensor.matmul(bank(4), C("ones"), sqsum[:, :], start=True, stop=True).then_inc(r2_sum, 1)
            pe.wait_ge(h2_lo, KT)

            with pe.Fori(0, FCH) as ch:
                with pe.Fori(0, FPC) as f:
                    for c in range(2):
                        pe.wait_ge(acc_read[(TN_FFN + c) % 2], (TN_CHUNK // 2) * ch + f + (TN_FFN + c - 2) // 2 + 1)
                        for q in range(4):
                            quarter(QN_FFN + 4 * c + q, QN_CHUNK * ch + 8 * f + (QN_FFN + 4 * c + q), (TN_FFN + c) % 2,
                                    hhi, hlo, range(4 * q, 4 * q + 4), q == 0, q == 3)
                with pe.Fori(0, KT // 2) as d:
                    for c in range(2):
                        pe.wait_ge(acc_read[(TN_FFN + c) % 2],
                                   (TN_CHUNK // 2) * ch + d + (TN_FFN + 2 * FPC + c - 2) // 2 + 1)
                        for q, (k0, kn) in enumerate(DOWN_K):
                            pe.wait_ge(a_lo, FPC * ch + (FPC if q == 3 else FPC - 1))
                            n = QN_FFN + 8 * FPC + 4 * c + q
                            quarter(n, QN_CHUNK * ch + 8 * d + n, (TN_FFN + c) % 2, ahi, alo,
                                    range(k0, k0 + kn), q == 0, q == 3)

        @block.scalar
        def _(sc):
            ch_ = Chain(sc, act_step)
            A = nc.scalar.activation

            def high(slot, n, loads, width=T):
                sc.wait_ge(raw_loaded[slot % NRAW], 16 * loads)
                if not isinstance(n, int) or n >= NW:
                    sc.wait_ge(w_used, n - NW + 1)
                A(whi[:, slot % NW, 0:width], raw[:, slot % NRAW, 0:width], ACT.Copy).then_inc(hi_ready, 1)

            def rsqrt(dst, src, scale, done):
                nc.scalar.preload_act_table_set("natural_log_exp_and_others")
                ch_.link(A(dst, src, ACT.Ln, bias=par("eps"), scale=scale))
                A(dst, dst, ACT.Exp, scale=-0.5).then_inc(done, 1)

            def side(t, q):
                a = 4 * t + q
                kind, j, _ = TILES[t - 1] if 0 < t <= NPROJ else ("", 0, 0)
                if kind in ("q", "k") and q == 0:
                    m = j + (4 if kind == "k" else 0)
                    wait_read(sc, t - 1)
                    if m >= 2:
                        sc.wait_ge(nq_sum, m - 1)
                    A(nsq[:, m % 2, :], qkT[:, m, :], ACT.Square).then_inc(nq_sq, 1)
                if kind == "z" and q == 0:
                    wait_read(sc, t - 1)
                    A(zs[:, j % 2, :], zs[:, j % 2, :], ACT.Silu).then_inc(z_silu, 1)
                if kind == "conv" and q == 1:
                    sc.wait_ge(conv_done, j + 1)
                    if j > 4:
                        sc.wait_ge(y_done, j - 4)
                    dst = bT[:, j, :] if j < 2 else cT[:, j - 2, :] if j < 4 else xsT
                    ci = 8 + j if j < 4 else j - 4
                    A(dst, cacc, ACT.Silu, bias=par("cb", ci)).then_inc(conv_silu, 1)
                if (t, q) == (1, 0):
                    sc.wait_ge(rows_ready, 1)
                    A(rrow, ps[0:HEADS, 4, 0:384], ACT.Copy).then_inc(rows_copied, 1)
                    A(far, ps[:, 5, 0:HEADS], ACT.Copy).then_inc(rows_copied, 1)
                if (t, q) == (2, 1):
                    wait_read(sc, 0)
                    sc.dma_start(ki_hi[64:128, :], misc[0:64, :]).then_inc(ki_dup, 16)
                    sc.wait_ge(rows_copied, 2)
                    sc.dma_start(bias_rows.rearrange("r h x -> h r x"),
                                 rrow.unsqueeze(1).to_broadcast([HEADS, P, 384])).then_inc(rows_stored, 16)
                if (t, q) == (2, 3):
                    sc.wait_ge(sp_in, 1)
                    A(sp[1], sp[0], ACT.Exp).then_inc(sp_exp, 1)
                    A(ealog, par("alog", 0, 16), ACT.Exp).then_inc(sp_exp, 1)
                if (t, q) == (4, 3):
                    sc.wait_ge(acs_diff, 1)
                    A(acs_row, ps[0:64, 3, 0:P], ACT.Copy).then_inc(acs_copied, 1)
                    A(total, ps[:, 3, P + 64:P + 128], ACT.Exp).then_inc(acs_copied, 1)
                    sc.wait_ge(acs_copied, 2)
                    sc.dma_start(acs_rows.rearrange("h c l -> (h c) l"), acs_row).then_inc(acs_stored, 16)
                if (t, q) == (5, 0):
                    sc.wait_ge(acs_diff, 1)
                    A(to_end, to_end, ACT.Exp).then_inc(acs_exp, 1)
                if (t, q) == (27, 0) or (t >= 29 and (t - 29) % 2 == 0 and (t - 29) // 2 < 7 and q == 0):
                    j2 = (t - 27) // 2
                    if j2 == 0:
                        sc.wait_ge(acs_stored, 16)
                    else:
                        sc.wait_ge(seg_ready, j2)
                        sc.wait_ge(lt_ready, j2)
                    sc.dma_start(rows.rearrange("p h c l -> p (h c l)"),
                                 acs_rows[2 * j2:2 * j2 + 2].rearrange("(a h) c l -> a (h c l)", a=1).to_broadcast([P, 8 * P])
                                 ).then_inc(rows_loaded, 16)
                if (t, q) == (3, 0):
                    sc.wait_ge(rows_stored, 16)
                    sc.wait_ge(h_lo, KT)
                    sc.dma_start(btile, bass.AP(bias_rows.tensor, P - 1, [[HEADS * 384 - 1, P], [384, HEADS], [1, 2 * P]])
                                 ).then_inc(btile_loaded, 16)
                if kind in ("q", "k") and q == 2:
                    m = j + (4 if kind == "k" else 0)
                    sc.wait_ge(nq_sum, m + 1)
                    if m:
                        sc.wait_ge(nq_done, m)
                    rsqrt(nrs, bank(4 + m % 2), 1.0 / 64, nq_r0)
                if IDX_AT <= a < IDX_AT + N_IDX // 2:
                    for e in (2 * (a - IDX_AT), 2 * (a - IDX_AT) + 1):
                        b = 1 + e // HEADS
                        sc.wait_ge(idx_s, e + 1)
                        if e >= 2:
                            sc.wait_ge(idx_acc, e - 1)
                        A(relu[:, e % 2, 0:P * (b + 1)], ps[:, 2 + e % 2, 0:P * (b + 1)], ACT.Relu).then_inc(idx_relu, 1)
                if ATT_AT <= a < ATT_AT + N_ATT + 3:
                    u = a - ATT_AT
                    if u < N_ATT:
                        b = u % NCH
                        sc.wait_ge(att_max, u + 1)
                        x = logit[:, u % 4, 0:P * (b + 1)]
                        A(x, x, ACT.Exp, bias=nmax[:, u % 4:u % 4 + 1], accum_out=rsum[:, u % 4:u % 4 + 1]).then_inc(att_exp, 1)
                    u = a - ATT_AT - 2
                    if 0 <= u < N_ATT:
                        b = u % NCH
                        sc.wait_ge(att_t, u + 1)
                        if u >= 2:
                            sc.wait_ge(att_pv, u - 1)
                        A(pT[:, u % 2, 0:P * (b + 1)], ps[:, 4 + u % 2, 0:P * (b + 1)], ACT.Copy).then_inc(att_pt, 1)
                    u = a - ATT_AT - 3
                    if 0 <= u < N_ATT and u % 8 == 7:
                        sc.wait_ge(att_pv, u + 1)
                        A(resid[:, 8 + u // 8, :], bank(6 + (u // 8) % 2), ACT.Copy).then_inc(att_out, 1)
                if t >= 28 and (t - 28) % 2 == 0 and (t - 28) // 2 < 8 and q == 2:
                    j2 = (t - 28) // 2
                    sc.wait_ge(rows_loaded, 16 * (j2 + 1))
                    if j2:
                        sc.wait_ge(y_ready, j2)
                    A(ce.rearrange("p h c l -> p h (c l)"), rows[:, :, 1:4, :].rearrange("p h c l -> p h (c l)"), ACT.Exp)
                    sc.wait_ge(seg_ready, j2 + 1)
                    g1 = gmat.rearrange("p h c l -> p (h c l)")
                    A(g1, g1, ACT.Exp).then_inc(lt_ready, 1)
                if (t, q) in ((36, 3), (44, 3)):
                    sc.wait_ge(gn_sum, 1 if t == 36 else 2)
                    rsqrt(nrs, bank(7), 1.0 / 512, gn_r0)
                if SPLIT_AT <= a < SPLIT_AT + 16:
                    split_high(a - SPLIT_AT)
                if (t, q) == (48, 3):
                    for i in range(6):
                        reload(i)

            def split_high(k):
                if k == 0:
                    sc.wait_ge(gn_done, 2)
                    sc.wait_ge(sc_done, 3)
                if k == 15:
                    sc.wait_ge(sc_done, 4)
                A(yhi[:, k, :], resid[:, k, :], ACT.Copy).then_inc(y_hi, 1)

            def reload(i):
                sc.wait_ge(y_lo, 2 * i + 2)
                sc.dma_start(resid[:, 2 * i:2 * i + 2, :], xT[:, 2 * i:2 * i + 2, :]).then_inc(x_loaded[i], 16)

            sc.dma_start(pc[:, :], params).then_inc(par_loaded, 16)
            for i in range(8):
                sc.dma_start(resid[:, 2 * i:2 * i + 2, :], xT[:, 2 * i:2 * i + 2, :]).then_inc(x_loaded[i], 16)
            sc.dma_start(oneh_t, onehot).then_inc(const_loaded, 16)
            sc.dma_start(relt, relb).then_inc(const_loaded, 16)
            sc.dma_start(cm[:, :, :], cmats).then_inc(const_loaded, 16)
            nc.scalar.preload_act_table_set("natural_log_exp_and_others")
            sc.wait_ge(par_loaded, 16)
            for k in range(KT):
                if k % 4 == 0:
                    high(k // 4, k // 4, 1)
                if k % 2 == 0:
                    sc.wait_ge(x_loaded[k // 2], 16)
                A(hhi[:, k, :], resid[:, k, :], ACT.Copy, scale=par("gmix", k)).then_inc(h_hi, 1)
            for k in range(0, KT, 2):
                if k:
                    if k >= 6:
                        sc.wait_ge(x_acc, k - 4)
                    A(nsq[:, (k // 2) % 2, :], resid[:, k, :], ACT.Square).then_inc(x_sq, 1)
                else:
                    A(sqsum[:, :], resid[:, 0, :], ACT.Square).then_inc(x_sq, 1)
                if k % 4 == 0:
                    high(4 + k // 4, 4 + k // 4, 2)
            sc.wait_ge(x_sum, 1)
            rsqrt(sqsum[:, :], bank(2), 1.0 / D, x_r0)

            for t in range(2, NPROJ + 2):
                for q in range(4):
                    high(4 * t + q, 4 * t + q, t + 1)
                    side(t - 1, q)

            reload(6)
            reload(7)

            def residual(d, n):
                sc.wait_ge(acc_read[(TN_OUT + n[1]) % 2], n[2])
                sc.wait_ge(x2_sum, n[0])
                A(bank(2 + n[1]), resid_block(d), ACT.Square).then_inc(x2_sq, 1)
                A(hhi_block(d), resid_block(d), ACT.Copy, scale=pc[:, bass.ds(d + PC["gffn"], 1)]).then_inc(h2_hi, 1)

            def resid_block(d):
                return resid[:, bass.ds(d, 1), :].rearrange("p a t -> p (a t)")

            def hhi_block(d):
                return hhi[:, bass.ds(d, 1), :].rearrange("p a t -> p (a t)")

            def highs(q0, n0, e, coef, width=(T,) * 4):
                for q in range(q0, q0 + 4):
                    n = n0 + q
                    high(n, e + n, coef + (n // 4 + 1), width[q % 4])

            with sc.Fori(1, KT // 2) as i:
                highs(0, QN_OUT, 8 * i, 2 * i)
                residual(2 * i - 2, (2 * i - 1, 0, i + TN_OUT // 2))
                highs(4, QN_OUT, 8 * i, 2 * i)
                residual(2 * i - 1, (2 * i, 1, i + (TN_OUT + 1) // 2))

            DW = [kn * P for _, kn in DOWN_K]

            def silu(n):
                sc.wait_ge(f_conv, n)
                A(gsilu[:, :], gconv[:, :], ACT.Silu).then_inc(f_silu, 1)

            def act_high(f, n):
                sc.wait_ge(f_act, n)
                A(ahi[:, bass.ds(f, 1), :].rearrange("p a t -> p (a t)"), act[:, :], ACT.Copy).then_inc(a_hi, 1)

            def mlp_chunk(c, first=False, last=False):
                e0, c0 = QN_CHUNK * c, (QN_CHUNK // 4) * c
                highs(0, QN_FFN, e0, c0)
                if first:
                    residual(KT - 2, (KT - 1, 0, KT // 2 + TN_OUT // 2))
                highs(4, QN_FFN, e0, c0)
                if first:
                    residual(KT - 1, (KT, 1, KT // 2 + (TN_OUT + 1) // 2))
                    sc.wait_ge(r2_sum, 1)
                    rsqrt(rstd2[:, :], bank(4), 1.0 / D, r2_r0)
                with sc.Fori(1, FPC) as f:
                    highs(0, QN_FFN, e0 + 8 * f, c0 + 2 * f)
                    silu(FPC * c + f)
                    highs(4, QN_FFN, e0 + 8 * f, c0 + 2 * f)
                    act_high(f - 1, FPC * c + f)
                q0 = QN_FFN + 8 * FPC
                highs(0, q0, e0, c0, DW)
                silu(FPC * c + FPC)
                highs(4, q0, e0, c0, DW)
                act_high(FPC - 1, FPC * c + FPC)
                with sc.Fori(1, KT // 2) as d:
                    highs(0, q0, e0 + 8 * d, c0 + 2 * d, DW)
                    if last:
                        store(2 * d - 2, 0, d)
                    highs(4, q0, e0 + 8 * d, c0 + 2 * d, DW)
                    if last:
                        store(2 * d - 1, 1, d)

            def store(d, parity, n):
                t0 = TN_FFN + TN_CHUNK * (FCH - 1) + 2 * FPC + parity
                sc.wait_ge(acc_read[t0 % 2], t0 // 2 + n)
                sc.dma_start(out[bass.ds(d, 1), :, :].rearrange("a p t -> (a p) t"), resid_block(d)).then_inc(out_stored, 16)

            mlp_chunk(0, first=True)
            with sc.Fori(1, FCH - 1) as c:
                mlp_chunk(c)
            mlp_chunk(FCH - 1, last=True)
            store(KT - 2, 0, KT // 2)
            store(KT - 1, 1, KT // 2)
            sc.wait_ge(out_stored, 16 * KT)

        @block.vector
        def _(ve):
            V = nc.vector
            ch_ = Chain(ve, vec)

            def newton(r, t, total, n):
                ch_.link(V.scalar_tensor_tensor(t, total, EPS * n, r, ALU.add, ALU.mult))
                ch_.link(V.scalar_tensor_tensor(t, t, -0.5 / n, r, ALU.mult, ALU.mult))
                ch_.link(V.scalar_tensor_tensor(r, t, 1.5, r, ALU.add, ALU.mult))

            def read_out(t):
                kind, j, _ = TILES[t]
                m = j + (4 if kind == "k" else 0)
                wait_tile(ve, t)
                if kind == "q" and j == 0:
                    ve.wait_ge(dt_ready, 1)
                if kind == "v" and j >= 2:
                    ve.wait_ge(v_tr, j - 1)
                if kind in ("scb", "scc", "sch") and j:
                    ve.wait_ge(sc_done, j)
                if kind == "conv" and j:
                    ve.wait_ge(conv_done, j)
                if kind == "z" and j >= 2:
                    ve.wait_ge(y_done, j - 1)
                dst = {"misc": lambda: misc, "qi": lambda: qi[:, j, :], "q": lambda: qkT[:, m, :], "k": lambda: qkT[:, m, :],
                       "v": lambda: vT[:, j % 2, :], "scb": lambda: scb, "scc": lambda: scm[:, 2:], "sch": lambda: scm[:, 2:],
                       "conv": lambda: cpad[:, 3:], "z": lambda: zs[:, j % 2, :]}[kind]()
                if kind == "sch":
                    wait_read(ve, t - 1)
                    V.tensor_tensor(dst, bank(t % 2), dst, ALU.mult).then_inc(acc_read[t % 2], 1)
                    wait_read(ve, t)
                    ch_.link(V.tensor_tensor(dst, dst, sqsum[:, :], ALU.mult))
                else:
                    V.tensor_tensor(dst, bank(t % 2), sqsum[:, :], ALU.mult).then_inc(acc_read[t % 2], 1)

            def side(t, q):
                a = 4 * t + q
                kind, j, _ = TILES[t - 1] if 0 < t <= NPROJ else ("", 0, 0)
                if (t, q) == (2, 0):
                    read_out(0)
                if q == 0 and t >= 2 and kind:
                    read_out(t - 1)
                if (t, q) == (2, 2):
                    ve.wait_ge(misc_tok, 1)
                    m3 = bank(3).rearrange("p (c n) -> p c n", c=4)
                    V.tensor_copy(widx, m3[:, :, M_WI:M_WI + HEADS])
                    V.tensor_tensor(sp[2], m3[:, :, M_DT:M_DT + SSD_HEADS],
                                    par("dtb", 0, 16).unsqueeze(1).to_broadcast([P, 4, SSD_HEADS]), ALU.add).then_inc(misc_used, 1)
                    ve.wait_ge(misc_used, 1)
                    V.scalar_tensor_tensor(sp[0], sp[2], -1.0, sp[2], ALU.mult, ALU.min).then_inc(sp_in, 1)
                if (t, q) == (3, 0):
                    ve.wait_ge(sp_exp, 2)
                    u, x, den, z2, p = sp[1], sp[2], sp[3], sp[4], sp[5]
                    ch_.link(V.tensor_scalar(den, u, 2.0, None, ALU.add))
                    ch_.link(V.reciprocal(den, den))
                    ch_.link(V.tensor_tensor(u, u, den, ALU.mult))
                    ch_.link(V.tensor_tensor(z2, u, u, ALU.mult))
                    ch_.link(V.tensor_scalar(p, z2, LOG1P[8], None, ALU.mult))
                    for i in range(7, 0, -1):
                        ch_.link(V.scalar_tensor_tensor(p, p, LOG1P[i], z2, ALU.add, ALU.mult))
                    ch_.link(V.scalar_tensor_tensor(p, p, 1.0, u, ALU.add, ALU.mult))
                    ch_.link(V.tensor_scalar(x, x, 0.0, None, ALU.max))
                    ch_.link(V.scalar_tensor_tensor(dt, p, 2.0, x, ALU.mult, ALU.add))
                    V.scalar_tensor_tensor(dta.rearrange("p (h c) -> p c h", h=SSD_HEADS), dt, -1.0, ealog.unsqueeze(1).to_broadcast([P, 4, SSD_HEADS]),
                                           ALU.mult, ALU.mult).then_inc(dt_ready, 1)
                if (t, q) == (4, 2):
                    ve.wait_ge(acs_sum, 1)
                    ch_.link(V.tensor_copy(acs, ps[:, 3, P:P + 64]))
                    V.tensor_tensor(to_end, ps[:, 3, P + 64:P + 128], acs, ALU.subtract).then_inc(acs_diff, 1)
                if kind in ("q", "k") and q == 3:
                    m = j + (4 if kind == "k" else 0)
                    ve.wait_ge(nq_r0, m + 1)
                    newton(nrs, ntmp, bank(4 + m % 2), 64)
                    wait_read(ve, t - 1)
                    V.scalar_tensor_tensor(qkT[:, m, :], qkT[:, m, :], par("g" + kind), nrs, ALU.mult, ALU.mult).then_inc(nq_done, 1)
                if kind == "v" and q == 2:
                    ve.wait_ge(v_tr, j + 1)
                    V.tensor_copy(vtok[:, :, j * P:(j + 1) * P], bank(6 + j % 2).rearrange("p (c d) -> p c d", c=4)).then_inc(v_tok, 1)
                if IDX_AT <= a < IDX_AT + N_IDX // 2:
                    for e in (2 * (a - IDX_AT), 2 * (a - IDX_AT) + 1):
                        b, h = 1 + e // HEADS, e % HEADS
                        ve.wait_ge(idx_relu, e + 1)
                        r = relu[:, e % 2, 0:P * (b + 1)]
                        if h == 0:
                            V.tensor_scalar(score[b], r, widx[:, b, h:h + 1], None, ALU.mult).then_inc(idx_acc, 1)
                        else:
                            ve.wait_ge(idx_acc, e)
                            V.scalar_tensor_tensor(score[b], r, widx[:, b, h:h + 1], score[b], ALU.mult, ALU.add).then_inc(idx_acc, 1)
                        if h == HEADS - 1:
                            ve.wait_ge(idx_acc, e + 1)
                            ch_.link(V.tensor_tensor(score[b][:, b * P:], score[b][:, b * P:], C("causal"), ALU.add))
                if TOPK_AT <= a < TOPK_AT + N_ROUND // 2:
                    for r in (2 * (a - TOPK_AT), 2 * (a - TOPK_AT) + 1):
                        b, last = 1 + r // (TOPK // 8), r % (TOPK // 8) == TOPK // 8 - 1
                        ch_.link(V.max(top8, score[b]))
                        ch_.link(V.match_replace(score[b], top8, score[b], TAKEN))
                        if last:
                            V.tensor_scalar(score[b], score[b], 0.5 * TAKEN, NEG, ALU.is_gt, ALU.mult).then_inc(mask_ready, 1)
                if ATT_AT <= a < ATT_AT + N_ATT + 3:
                    u = a - ATT_AT - 1
                    if 0 <= u < N_ATT:
                        b, s = u % NCH, slice(u % 4, u % 4 + 1)
                        ve.wait_ge(att_exp, u + 1)
                        ch_.link(V.reciprocal(rinv[:, s], rsum[:, s]))
                        x = logit[:, u % 4, 0:P * (b + 1)]
                        V.tensor_scalar(x, x, rinv[:, s], None, ALU.mult).then_inc(att_p, 1)
                    u = a - ATT_AT
                    if u < N_ATT:
                        h, b, s = u // NCH, u % NCH, slice(u % 4, u % 4 + 1)
                        if u == 0:
                            ve.wait_ge(btile_loaded, 16)
                            ve.wait_ge(acs_stored, 16)
                            ve.wait_ge(mask_ready, 3)
                        ve.wait_ge(att_s, u + 1)
                        if u >= 4:
                            ve.wait_ge(att_t, u - 3)
                        x, near = logit[:, u % 4, 0:P * (b + 1)], P * max(b - 1, 0)
                        if near:
                            V.tensor_scalar(x[:, 0:near], ps[:, 2 + u % 2, 0:near], 0.125, far[:, h:h + 1], ALU.mult, ALU.add)
                        V.scalar_tensor_tensor(x[:, near:], ps[:, 2 + u % 2, near:P * (b + 1)], 0.125,
                                               btile[:, h, (P if b == 0 else 0):2 * P], ALU.mult, ALU.add).then_inc(att_log, 1)
                        ve.wait_ge(att_log, u + 1)
                        ch_.link(V.tensor_tensor_reduce(out=x, in0=x, in1=C("causal") if b == 0 else score[b], scale=1.0,
                                                        scalar=TAKEN, op0=ALU.add, op1=ALU.max, accum_out=rmax[:, s]))
                        V.tensor_scalar(nmax[:, s], rmax[:, s], -1.0, None, ALU.mult).then_inc(att_max, 1)
                if kind == "sch" and q == 0:
                    ch_.link(V.tensor_scalar(scu, scm[:, 2:], par("scw", 3 * j + 2), None, ALU.mult))
                    ch_.link(V.scalar_tensor_tensor(scu, scm[:, 1:T + 1], par("scw", 3 * j + 1), scu, ALU.mult, ALU.add))
                    ch_.link(V.scalar_tensor_tensor(scu, scm[:, 0:T], par("scw", 3 * j), scu, ALU.mult, ALU.add))
                    V.tensor_tensor(resid[:, 12 + j, :], scu, scb, ALU.mult).then_inc(sc_done, 1)
                if kind == "conv" and q == 0:
                    wait_read(ve, t - 1)
                    if j:
                        ve.wait_ge(conv_silu, j)
                    ci = 8 + j if j < 4 else j - 4
                    ch_.link(V.tensor_scalar(cacc, cpad[:, 3:], par("cw", 4 * ci + 3), None, ALU.mult))
                    for i in (2, 1):
                        ch_.link(V.scalar_tensor_tensor(cacc, cpad[:, i:i + T], par("cw", 4 * ci + i), cacc, ALU.mult, ALU.add))
                    V.scalar_tensor_tensor(cacc, cpad[:, 0:T], par("cw", 4 * ci), cacc, ALU.mult, ALU.add).then_inc(conv_done, 1)
                if (t, q) == (28, 0):
                    ve.wait_ge(bc_prep, 1)
                    for g in range(2):
                        V.tensor_copy(btok[:, g, :, :].rearrange("p c n -> p (c n)"), bank(6 + g))
                        ins = V.tensor_tensor(cbt[:, g, :, :], bank(2 + g).rearrange("p (c l) -> p c l", c=4),
                                              C("triu").unsqueeze(1).to_broadcast([P, 4, P]), ALU.mult)
                    ins.then_inc(bc_done, 1)
                if t >= 28:
                    if (t - 28) % 2 == 0 and (t - 28) // 2 < 8:
                        j2 = (t - 28) // 2
                        g = j2 // 4
                        if q == 1:
                            ve.wait_ge(rows_loaded, 16 * (j2 + 1))
                            if j2:
                                ve.wait_ge(y_ready, j2)
                            acs_s = acs[:, 8 * j2:8 * j2 + 8].rearrange("p (h c) -> p h c", h=2).unsqueeze(3).to_broadcast([P, 2, 4, P])
                            ch_.link(V.tensor_tensor(gmat, rows, acs_s, ALU.min))
                            V.tensor_tensor(gmat, gmat, acs_s, ALU.subtract).then_inc(seg_ready, 1)
                        if q == 3:
                            ve.wait_ge(lt_ready, j2 + 1)
                            if j2 == 0:
                                ve.wait_ge(bc_done, 1)
                            V.tensor_tensor(gmat, gmat, cbt[:, g:g + 1, :, :].to_broadcast([P, 2, 4, P]), ALU.mult)
                            V.tensor_tensor(ce, ce, cT[:, g, P:T].rearrange("p (c l) -> p c l", c=3).unsqueeze(1).to_broadcast([P, 2, 3, P]),
                                            ALU.mult).then_inc(g_ready, 1)
                    if (t - 29) % 2 == 0 and 0 <= (t - 29) // 2 < 8:
                        j2 = (t - 29) // 2
                        if q == 2:
                            ve.wait_ge(xs_tr, j2 + 1)
                            ve.wait_ge(acs_exp, 1)
                            ch_.link(V.tensor_tensor(xdt, bank(6).rearrange("p (c h d) -> p c h d", c=4, h=2),
                                                     dt[:, :, 2 * j2:2 * j2 + 2].unsqueeze(3).to_broadcast([P, 4, 2, 64]), ALU.mult))
                            V.tensor_tensor(xdd, xdt[:, 0:3, :, :], to_end[:, 8 * j2:8 * j2 + 8].rearrange("p (h c) -> p c h", h=2)[:, 0:3, :]
                                            .unsqueeze(3).to_broadcast([P, 3, 2, 64]),
                                            ALU.mult).then_inc(xdt_ready, 1)
                        if q == 3:
                            ve.wait_ge(st_ready, j2 + 1)
                            b6 = bank(6).rearrange("p (c h d) -> p c h d", c=4, h=2)
                            ch_.link(V.tensor_copy(hst[:, 0, :, :], b6[:, 0, :, :]))
                            for c in (1, 2):
                                for hh in range(2):
                                    ins = V.scalar_tensor_tensor(hst[:, c, hh, :], hst[:, c - 1, hh, :], total[:, 4 * (2 * j2 + hh) + c:4 * (2 * j2 + hh) + c + 1],
                                                                 b6[:, c, hh, :], ALU.mult, ALU.add)
                                    if c == 1:
                                        ch_.link(ins)
                            ins.then_inc(hst_ready, 1)
                    if (t - 30) % 2 == 0 and 0 <= (t - 30) // 2 < 8 and q == 1:
                        j2 = (t - 30) // 2
                        y = resid[:, j2, :]
                        ve.wait_ge(y_ready, j2 + 1)
                        ch_.link(V.scalar_tensor_tensor(y, xsT, par("dskip", j2), bank(7), ALU.mult, ALU.add))
                        ve.wait_ge(z_silu, j2 + 1)
                        ch_.link(V.tensor_tensor(y, y, zs[:, j2 % 2, :], ALU.mult))
                        if j2 % 4 == 0:
                            V.tensor_tensor(gsum, y, y, ALU.mult).then_inc(y_done, 1)
                        else:
                            ch_.link(V.tensor_tensor(gtmp, y, y, ALU.mult))
                            V.tensor_tensor(gsum, gsum, gtmp, ALU.add).then_inc(y_done, 1)
                    if (t, q) in ((37, 0), (45, 0)):
                        g = 0 if t == 37 else 1
                        ve.wait_ge(gn_r0, g + 1)
                        newton(nrs, ntmp, bank(7), 512)
                    if (t, q) in ((37, 1), (45, 1)):
                        g = 0 if t == 37 else 1
                        for j3 in range(4 * g, 4 * g + 4):
                            ins = V.scalar_tensor_tensor(resid[:, j3, :], resid[:, j3, :], par("gssd", j3), nrs, ALU.mult, ALU.mult)
                        ins.then_inc(gn_done, 1)
                if SPLIT_AT <= a < SPLIT_AT + 16:
                    k = a - SPLIT_AT
                    ve.wait_ge(y_hi, k + 1)
                    if k == 12:
                        ve.wait_ge(sc_done, 4)
                    V.tensor_tensor(ylo[:, k, :], resid[:, k, :], yhi[:, k, :].bitcast(F32), ALU.subtract).then_inc(y_lo, 1)

            ve.wait_ge(par_loaded, 16)
            for k in range(KT):
                ve.wait_ge(h_hi, k + 1)
                V.scalar_tensor_tensor(hlo[:, k, :], resid[:, k, :], par("gmix", k), hhi[:, k, :].bitcast(F32),
                                       ALU.mult, ALU.subtract).then_inc(h_lo, 1)
            for k in range(KT):
                if k >= 2:
                    ve.wait_ge(x_acc, k - 1)
                if k % 2:
                    ch_.link(V.tensor_tensor(ntmp, resid[:, k, :], resid[:, k, :], ALU.mult))
                    term = ntmp
                else:
                    ve.wait_ge(x_sq, k // 2 + 1)
                    term = nsq[:, (k // 2) % 2, :]
                if k:
                    V.tensor_tensor(sqsum[:, :], sqsum[:, :], term, ALU.add).then_inc(x_acc, 1)
            ve.wait_ge(x_r0, 1)
            newton(sqsum[:, :], ntmp, bank(2), D)
            V.memset(scm[:, 0:2], 0.0)

            for t in range(NPROJ + 1):
                for q in range(4):
                    if (t, q) == (23, 0):
                        V.memset(cpad[:, 0:3], 0.0)
                    side(t, q)

            def blk(x, d):
                return x[:, bass.ds(d, 1), :].rearrange("p a t -> p (a t)")

            def residual(d, c, done, n):
                ve.wait_ge(w_used, done)
                V.tensor_tensor(blk(resid, d), bank((TN_OUT + c) % 2), blk(resid, d), ALU.add).then_inc(acc_read[(TN_OUT + c) % 2], 1)
                ve.wait_ge(x2_sq, n)
                ve.wait_ge(x2_sum, n)
                V.tensor_tensor(sqsum[:, :], sqsum[:, :], bank(2 + c), ALU.add).then_inc(x2_sum, 1)
                ve.wait_ge(h2_hi, n)
                V.scalar_tensor_tensor(blk(hlo, d), blk(resid, d), pc[:, bass.ds(d + PC["gffn"], 1)], blk(hhi, d).bitcast(F32),
                                       ALU.mult, ALU.subtract).then_inc(h2_lo, 1)

            V.memset(sqsum[:, :], 0.0).then_inc(x2_sum, 1)
            ve.wait_ge(x_loaded[0], 32)
            for c in range(2):
                residual(c, c, QN_OUT + 4 * c + 4, c + 1)
            for i in range(1, 8):
                ve.wait_ge(x_loaded[i], 32)
            with ve.Fori(1, KT // 2) as i:
                for c in range(2):
                    residual(2 * i + c, c, 8 * i + (QN_OUT + 4 * c + 4), 2 * i + (c + 1))

            ve.wait_ge(r2_r0, 1)
            newton(rstd2[:, :], ntmp2[:, :], bank(4), D)
            ch_.link(V.memset(gpad[:, 0:2], 0.0))
            links = ch_.n
            per_f = 2

            with ve.Fori(0, FCH) as c:
                with ve.Fori(0, FPC) as f:
                    ch_.n, ch_.base = 0, per_f * FPC * c + per_f * f + links
                    q0 = QN_CHUNK * c + 8 * f + QN_FFN
                    count = FPC * c + f
                    taps = [pc[:, bass.ds(3 * FPC * c + 3 * f + (PC["fcw"] + i), 1)] for i in range(3)]
                    ve.wait_ge(w_used, q0 + 4)
                    V.tensor_tensor(gpad[:, 2:], bank(TN_FFN % 2), rstd2[:, :], ALU.mult).then_inc(acc_read[TN_FFN % 2], 1)
                    ve.wait_ge(acc_read[TN_FFN % 2], (TN_CHUNK // 2) * c + f + (TN_FFN // 2 + 1))
                    ch_.link(V.tensor_scalar(gconv[:, :], gpad[:, 2:], taps[2], None, ALU.mult))
                    ch_.link(V.scalar_tensor_tensor(gconv[:, :], gpad[:, 1:T + 1], taps[1], gconv[:, :], ALU.mult, ALU.add))
                    V.scalar_tensor_tensor(gconv[:, :], gpad[:, 0:T], taps[0], gconv[:, :], ALU.mult, ALU.add).then_inc(f_conv, 1)
                    assert ch_.n == per_f
                    ve.wait_ge(w_used, q0 + 8)
                    par1 = (TN_FFN + 1) % 2
                    V.tensor_tensor(upv[:, :], bank(par1), rstd2[:, :], ALU.mult).then_inc(acc_read[par1], 1)
                    ve.wait_ge(acc_read[par1], (TN_CHUNK // 2) * c + f + ((TN_FFN + 1) // 2 + 1))
                    ve.wait_ge(f_silu, count + 1)
                    V.tensor_tensor(act[:, :], upv[:, :], gsilu[:, :], ALU.mult).then_inc(f_act, 1)
                    ve.wait_ge(f_act, count + 1)
                    ve.wait_ge(a_hi, count + 1)
                    V.tensor_tensor(blk(alo, f), act[:, :], blk(ahi, f).bitcast(F32), ALU.subtract).then_inc(a_lo, 1)
                with ve.Fori(0, KT // 2) as d:
                    for p in range(2):
                        ve.wait_ge(w_used, QN_CHUNK * c + 8 * d + (QN_FFN + 8 * FPC + 4 * p + 4))
                        V.tensor_tensor(blk(resid, 2 * d + p), bank((TN_FFN + p) % 2), blk(resid, 2 * d + p),
                                        ALU.add).then_inc(acc_read[(TN_FFN + p) % 2], 1)


def bucket_of(dist):
    n = np.maximum(dist, 0)
    exact = BUCKETS // 2
    large = exact + (np.log(np.maximum(n, exact).astype(np.float32) / np.float32(exact))
                     / np.float32(np.log(128 / exact)) * (BUCKETS - exact)).astype(np.int32)
    return np.where(n < exact, n, np.minimum(large, BUCKETS - 1))


def constants():
    i = np.arange(P)
    r, c = i[:, None], i[None, :]
    m = {"ident": r == c, "triu": r <= c, "after": r > c, "causal": np.where(c > r, NEG, 0.0),
         "ones": np.ones((P, P)), "halves": (r // 64) == (c // 64)}
    cm = np.stack([np.asarray(m[n], np.float32) for n in CM_NAMES], axis=1)
    oh = np.zeros((BUCKETS, 512), np.float32)
    oh[bucket_of(255 - np.arange(384)), np.arange(384)] = 1.0
    oh[BUCKETS - 1, 384:] = 1.0
    return np.ascontiguousarray(cm), oh


def lay_out(x, norm_mix, w_in, ssd_conv_w, ssd_conv_b, ssd_dt_bias, ssd_a_log, ssd_d, ssd_norm, att_q_norm, att_k_norm,
            rel_bias, sc_conv_w, w_out, norm_ffn, ffn_w_gate, ffn_w_up, ffn_conv_w, ffn_w_down):
    f = np.float32
    a = {}
    a["xT"] = np.ascontiguousarray(x[0].T.reshape(KT, P, T).transpose(1, 0, 2))
    w = w_in[0]
    cols = []
    for kind, j, at in TILES:
        if kind == "misc":
            m = np.zeros((D, P), f)
            m[:, M_KI:M_KI + 64] = w[:, OFF_KI:OFF_KI + 64]
            m[:, M_DT:M_DT + SSD_HEADS] = w[:, OFF_DT:OFF_DT + SSD_HEADS]
            m[:, M_WI:M_WI + HEADS] = w[:, OFF_WI:OFF_WI + HEADS]
            cols.append(m)
        else:
            cols.append(w[:, at:at + P])

    def tiles(blocks):
        return np.ascontiguousarray(np.stack([b.reshape(-1, P, P).transpose(1, 0, 2).reshape(P, -1) for b in blocks]))

    a["w_in"] = tiles(cols)
    a["w_out"] = tiles([w_out[0][:, d * P:(d + 1) * P] for d in range(KT)])
    a["w_gu"] = tiles([m[0][:, j * P:(j + 1) * P] for j in range(FT) for m in (ffn_w_gate, ffn_w_up)])
    rows = FPC * P
    a["w_dn"] = tiles([ffn_w_down[0][c * rows:(c + 1) * rows, d * P:(d + 1) * P] for c in range(FCH) for d in range(KT)])
    pc = np.zeros((P, NPC), f)

    def put(name, v):
        pc[:, PC[name]:PC[name] + v.shape[1]] = v

    def taps(v):
        k = v.shape[0]
        return v.reshape(k, -1, P).transpose(2, 1, 0).reshape(P, -1)

    put("gmix", norm_mix[0].reshape(-1, P).T)
    put("gffn", norm_ffn[0].reshape(-1, P).T)
    put("cw", taps(ssd_conv_w[0]))
    put("cb", ssd_conv_b[0].reshape(-1, P).T)
    put("scw", taps(sc_conv_w[0]))
    put("fcw", taps(ffn_conv_w[0]))
    put("dskip", np.repeat(ssd_d[0], 64).reshape(-1, P).T)
    put("gssd", ssd_norm[0].reshape(-1, P).T)
    put("gq", np.tile(att_q_norm[0], 2)[:, None])
    put("gk", np.tile(att_k_norm[0], 2)[:, None])
    put("dtb", np.tile(ssd_dt_bias[0][None, :], (P, 1)))
    put("alog", np.tile(ssd_a_log[0][None, :], (P, 1)))
    pc[:, PC["eps"]] = EPS
    a["params"] = pc
    a["relb"] = np.ascontiguousarray(rel_bias)
    a["cmats"], a["onehot"] = constants()
    return a


def kernel(**inputs):
    import concourse.bacc as bacc
    from concourse.bass_utils import run_bass_kernel_spmd as run

    f32 = mybir.dt.float32
    nc = bacc.Bacc("TRN2", target_bir_lowering=False, num_devices=1)
    arrays = lay_out(**{k: np.asarray(v) for k, v in inputs.items()})
    args = [nc.dram_tensor(n, v.shape, f32, kind="ExternalInput").ap() for n, v in arrays.items()]
    bias_rows = nc.dram_tensor("bias_rows", (P, HEADS, 384), f32, kind="Internal").ap()
    acs_rows = nc.dram_tensor("acs_rows", (SSD_HEADS, NCH, P), f32, kind="Internal").ap()
    out = nc.dram_tensor("outT", (KT, P, T), f32, kind="ExternalOutput").ap()
    hybrid_block(nc, *args, bias_rows, acs_rows, out)
    got = run(nc, [arrays], core_ids=[0]).results[0]["outT"]
    return np.ascontiguousarray(np.asarray(got).reshape(D, T).T).reshape(1, T, D)
```

```python
from contextlib import ExitStack

import numpy as np
import concourse.bass as bass
from concourse import mybir


P = 128
T = 512
D = 2048
KT = D // P
NCH = T // P
D_FF = 5632
FT = D_FF // P
FCH = 4
FPC = FT // FCH
HEADS = 8
SSD_HEADS = 16
TOPK = 128
BUCKETS = 32

D_SSD, D_ATT, D_SC = 1024, 512, 512
OFF_Z = 0
OFF_XS = OFF_Z + D_SSD
OFF_B = OFF_XS + D_SSD
OFF_C = OFF_B + 256
OFF_DT = OFF_C + 256
OFF_Q = OFF_DT + SSD_HEADS
OFF_K = OFF_Q + D_ATT
OFF_V = OFF_K + D_ATT
OFF_QI = OFF_V + D_ATT
OFF_KI = OFF_QI + 512
OFF_WI = OFF_KI + 64
OFF_SCB = OFF_WI + 8
OFF_SCC = OFF_SCB + D_SC
OFF_SCH = OFF_SCC + D_SC

M_KI, M_DT, M_WI = 0, 64, 96


def proj_tiles():
    tiles = [("misc", 0, None)]
    tiles += [("qi", j, OFF_QI + P * j) for j in range(4)]
    tiles += [("q", j, OFF_Q + P * j) for j in range(4)]
    tiles += [("k", j, OFF_K + P * j) for j in range(4)]
    tiles += [("v", j, OFF_V + P * j) for j in range(4)]
    for s in range(2):
        tiles += [("scb", s, OFF_SCB + P * s), ("scc", s, OFF_SCC + P * s), ("sch", s, OFF_SCH + P * s)]
    tiles += [("conv", j, OFF_B + P * j) for j in range(4)]
    for j in range(8):
        tiles += [("z", j, OFF_Z + P * j), ("conv", 4 + j, OFF_XS + P * j)]
    for s in range(2, 4):
        tiles += [("scb", s, OFF_SCB + P * s), ("scc", s, OFF_SCC + P * s), ("sch", s, OFF_SCH + P * s)]
    return tiles


TILES = proj_tiles()
NPROJ = len(TILES)
TILE_OF = {(kind, j): t for t, (kind, j, _) in enumerate(TILES)}

QN_OUT = 4 * NPROJ
QN_FFN = QN_OUT + 4 * KT
QN_CHUNK = 8 * FPC + 4 * KT
TN_OUT = NPROJ
TN_FFN = NPROJ + KT
TN_CHUNK = 2 * FPC + KT
NRAW, NW = 4, 8
DOWN_K = [(0, 3), (3, 3), (6, 3), (9, 2)]

PC_NAMES = [("gmix", 16), ("gffn", 16), ("cw", 48), ("cb", 12), ("scw", 12), ("fcw", 132), ("dskip", 8),
            ("gssd", 8), ("gq", 1), ("gk", 1), ("dtb", 16), ("alog", 16), ("eps", 1)]
PC = {}
_n = 0
for _name, _w in PC_NAMES:
    PC[_name] = _n
    _n += _w
NPC = _n

CM_NAMES = ["ident", "triu", "causal", "ones", "halves"]
NEG = -1.0e30
TAKEN = -3.0e38
EPS = 1e-6

IDX_AT = 4 * 5 + 2
TOPK_AT = IDX_AT + 4
ATT_AT = 4 * 17
SPLIT_AT = 4 * 46
XSUM_Q = 2
SQ_LAG = 2
WARM = 3
N_IDX = 3 * HEADS
N_ROUND = 3 * (TOPK // 8)
N_ATT = HEADS * NCH

LOG1P = [1.0 / (2 * i + 1) for i in range(9)]


def topk_rounds():
    quarter, rounds, r, a, room = 2450, {}, 0, TOPK_AT, 0
    while r < N_ROUND:
        kind, before, q = TILES[a // 4 - 1][0], TILES[a // 4 - 2][0], a % 4
        room = min(room, 1200) + quarter
        room -= 650 if q == 0 else 2900 if q == 1 and before in ("q", "k") else 650 if q == 2 and kind == "v" else 0
        room -= 900 if a < IDX_AT + N_IDX // 2 else 0
        rounds[a] = []
        while r < N_ROUND:
            b = 1 + r // (TOPK // 8)
            cost = 400 + 266 * (b + 1)
            if room < cost or a < IDX_AT + 4 * b - 1:
                break
            rounds[a].append(r)
            room -= cost
            r += 1
        a += 1
    assert a <= ATT_AT
    return rounds


def hybrid_block(nc, xT, w_in, w_out, w_gu, w_dn, params, relb, cmats, onehot, bias_rows, acs_rows, out):
    F32, F32R = mybir.dt.float32, mybir.dt.float32r
    ALU = mybir.AluOpType
    ACT = mybir.ActivationFunctionType

    with ExitStack() as ctx:
        def sb(name, shape, dt=F32):
            return ctx.enter_context(nc.sbuf_tensor(name, shape, dt))

        def sem(name):
            return ctx.enter_context(nc.semaphore(name))

        resid = sb("resid", [P, KT, T])
        hhi = sb("hhi", [P, KT, T], F32R)
        hlo = sb("hlo", [P, KT, T], F32R)
        raw = sb("raw", [P, NRAW, T])
        whi = sb("whi", [P, NW, T], F32R)
        wlo = sb("wlo", [P, NW, T], F32R)
        cm = sb("cm", [P, len(CM_NAMES), P])
        pc = sb("pc", [P, NPC])
        sqsum = sb("sqsum", [P, T])
        with ExitStack() as r:
            work = r.enter_context(nc.sbuf_tensor("work", [P, 32 * T], F32))
        with ExitStack() as r:
            yhi = r.enter_context(nc.sbuf_tensor("yhi", [P, KT, T], F32R))
            ylo = r.enter_context(nc.sbuf_tensor("ylo", [P, KT, T], F32R))
        with ExitStack() as r:
            ahi = r.enter_context(nc.sbuf_tensor("ahi", [P, FPC, T], F32R))
            alo = r.enter_context(nc.sbuf_tensor("alo", [P, FPC, T], F32R))
            rstd2 = r.enter_context(nc.sbuf_tensor("rstd2", [P, T], F32))
            ntmp2 = r.enter_context(nc.sbuf_tensor("ntmp2", [P, T], F32))
            gpad = r.enter_context(nc.sbuf_tensor("gpad", [P, T + 2], F32))
            gconv = r.enter_context(nc.sbuf_tensor("gconv", [P, T], F32))
            gsilu = r.enter_context(nc.sbuf_tensor("gsilu", [P, T], F32))
            upv = r.enter_context(nc.sbuf_tensor("upv", [P, T], F32))
            act = r.enter_context(nc.sbuf_tensor("act", [P, T], F32))

        def C(name):
            return cm[:, CM_NAMES.index(name), :]

        def par(name, j=0, n=1):
            return pc[:, PC[name] + j:PC[name] + j + n]

        def wk(at, n):
            return work[:, at:at + n]

        qi = wk(0, 2048).rearrange("p (j t) -> p j t", j=4)
        relu = wk(2048, 1024).rearrange("p (j t) -> p j t", j=2)
        misc = wk(3072, 512)
        ki_hi = wk(3584, 512)
        vT = wk(3072, 1024).rearrange("p (j t) -> p j t", j=2)
        nsq = wk(4096, 1024).rearrange("p (j t) -> p j t", j=2)
        pT = wk(4096, 1024).rearrange("p (j t) -> p j t", j=2)
        nrs = wk(5248, 512)
        ntmp = wk(5760, 512)
        qkT = wk(6272, 4096).rearrange("p (j t) -> p j t", j=8)
        zeros = qkT[:, 0, :]
        vtok = wk(10368, 2048).rearrange("p (c d) -> p c d", c=4)
        score_at = {1: 12416, 2: 12416 + 256, 3: 12416 + 640}
        score = {b: wk(score_at[b], P * (b + 1)) for b in (1, 2, 3)}
        rrow = work[0:HEADS, 13568:13568 + 384]
        small = 13952
        dt = wk(small, 64).rearrange("p (c h) -> p c h", c=4)
        dta = wk(small + 64, 64)
        widx = wk(small + 128, 32).rearrange("p (c h) -> p c h", c=4)
        far = wk(small + 160, 8)
        top8 = wk(small + 168, 8)
        rmax = wk(small + 176, 4)
        nmax = wk(small + 180, 4)
        rsum = wk(small + 184, 4)
        rinv = wk(small + 188, 4)
        acs = wk(small + 192, 64)
        to_end = wk(small + 256, 64)
        total = wk(small + 320, 64)
        ealog = wk(8084, 16)
        acs_row = resid[0:4 * SSD_HEADS, 7, 0:P]
        oneh_t = work[0:BUCKETS, 7168:7680]
        relt = work[0:BUCKETS, 7680:7688]
        sp = [wk(7700 + 64 * i, 64).rearrange("p (c h) -> p c h", c=4) for i in range(6)]
        scb = wk(14336, 512)
        scm = wk(14848, 514)
        scu = wk(15362, 512)
        cpad = wk(0, 515)
        cacc = wk(520, 512)
        bT = wk(1032, 1024).rearrange("p (g t) -> p g t", g=2)
        cT = wk(2056, 1024).rearrange("p (g t) -> p g t", g=2)
        btok = wk(3080, 1024).rearrange("p (g c n) -> p g c n", g=2, c=4)
        cbt = wk(4104, 1024).rearrange("p (g c l) -> p g c l", g=2, c=4)
        zs = wk(6272, 1024).rearrange("p (j t) -> p j t", j=2)
        xsT = wk(7296, 512)
        rows = wk(7808, 1024).rearrange("p (h c l) -> p h c l", h=2, c=4)
        gmat = wk(8832, 1024).rearrange("p (h c l) -> p h c l", h=2, c=4)
        ce = wk(9856, 768).rearrange("p (h c l) -> p h c l", h=2, c=3)
        xdt = wk(10624, 512).rearrange("p (c h d) -> p c h d", c=4, h=2)
        xdd = wk(11136, 384).rearrange("p (c h d) -> p c h d", c=3, h=2)
        hst = wk(11520, 384).rearrange("p (c h d) -> p c h d", c=3, h=2)
        gsum = wk(11904, 512)
        gtmp = wk(12416, 512)
        btile = resid[:, 0:4, :].rearrange("p a b -> p (a b)").rearrange("p (h k) -> p h k", h=HEADS)
        logit = resid[:, 4:8, :]

        ps = ctx.enter_context(nc.psum_tensor("ps", [P, 8, T], F32))

        def bank(i):
            return ps[:, i, :]

        def acc(t):
            return bank({2: 6, 3: 7}.get(t, t % 2))

        par_loaded, const_loaded = sem("par_loaded"), sem("const_loaded")
        x_loaded = [sem(f"x_loaded{i}") for i in range(8)]
        raw_loaded = [sem(f"raw_loaded{i}") for i in range(NRAW)]
        hi_ready, lo_ready, w_used = sem("hi_ready"), sem("lo_ready"), sem("w_used")
        acc_read = [sem("acc_read0"), sem("acc_read1")]
        x_sq, x_acc, x_r0 = sem("x_sq"), sem("x_acc"), sem("x_r0")
        h_hi, h_lo, x_sum = sem("h_hi"), sem("h_lo"), sem("x_sum")
        vec, act_step = sem("vec"), sem("act_step")
        rows_ready, rows_copied, rows_stored, btile_loaded = sem("rows_ready"), sem("rows_copied"), sem("rows_stored"), sem("btile_loaded")
        ki_dup, misc_tok, misc_used = sem("ki_dup"), sem("misc_tok"), sem("misc_used")
        sp_in, sp_exp, dt_ready = sem("sp_in"), sem("sp_exp"), sem("dt_ready")
        acs_sum, acs_copied, acs_diff, acs_exp = sem("acs_sum"), sem("acs_copied"), sem("acs_diff"), sem("acs_exp")
        acs_stored, rows_loaded = sem("acs_stored"), sem("rows_loaded")
        z_silu = sem("z_silu")
        idx_s, idx_relu, idx_acc = sem("idx_s"), sem("idx_relu"), sem("idx_acc")
        mask_ready = sem("mask_ready")
        nq_sq, nq_sum, nq_r0, nq_done = sem("nq_sq"), sem("nq_sum"), sem("nq_r0"), sem("nq_done")
        v_tr, v_tok = sem("v_tr"), sem("v_tok")
        att_s, att_log, att_max, att_exp = sem("att_s"), sem("att_log"), sem("att_max"), sem("att_exp")
        att_p, att_t, att_pt, att_pv, att_out = sem("att_p"), sem("att_t"), sem("att_pt"), sem("att_pv"), sem("att_out")
        sc_done = sem("sc_done")
        conv_done, conv_silu = sem("conv_done"), sem("conv_silu")
        bc_prep, bc_done = sem("bc_prep"), sem("bc_done")
        seg_ready, lt_ready, g_ready = sem("seg_ready"), sem("lt_ready"), sem("g_ready")
        xs_tr, xdt_ready, st_ready, hst_ready = sem("xs_tr"), sem("xdt_ready"), sem("st_ready"), sem("hst_ready")
        y_ready, y_done, gn_sum, gn_r0, gn_done = sem("y_ready"), sem("y_done"), sem("gn_sum"), sem("gn_r0"), sem("gn_done")
        y_hi, y_lo = sem("y_hi"), sem("y_lo")
        zeros_ready = sem("zeros_ready")
        x2_sq, x2_sum, h2_hi, h2_lo = sem("x2_sq"), sem("x2_sum"), sem("h2_hi"), sem("h2_lo")
        r2_sum, r2_r0 = sem("r2_sum"), sem("r2_r0")
        f_conv, f_silu, f_act, a_hi, a_lo = sem("f_conv"), sem("f_silu"), sem("f_act"), sem("a_hi"), sem("a_lo")
        out_stored = sem("out_stored")

        block = ctx.enter_context(nc.Block())

        class Chain:

            def __init__(self, eng, s):
                self.eng, self.s, self.n, self.base = eng, s, 0, 0

            def link(self, ins):
                self.n += 1
                ins.then_inc(self.s, 1)
                self.eng.wait_ge(self.s, self.base + self.n)

        def wait_tile(eng, t):
            eng.wait_ge(w_used, max(4 * (t + 1), 8))

        def wait_read(eng, t):
            eng.wait_ge(acc_read[t % 2], t // 2 + 1)

        def load_x(eng, i):
            eng.dma_start(resid[:, 2 * i:2 * i + 2, :], xT[:, 2 * i:2 * i + 2, :]).then_inc(x_loaded[i], 16)

        @block.sync
        def _(sp_):
            def load(slot, n, src, width):
                if not isinstance(n, int) or n >= NRAW:
                    sp_.wait_ge(lo_ready, n - NRAW + 1)
                sp_.dma_start(raw[:, slot % NRAW, 0:width], src).then_inc(raw_loaded[slot % NRAW], 16)

            for n in range(8):
                load(n, n, w_in[n % 2, :, n // 2 * T:(n // 2 + 1) * T], T)
                for i in {0: (0,), 1: (1,), 3: (2, 3), 5: (4, 5)}.get(n, ()):
                    load_x(sp_, i)
            load_x(sp_, 6)
            load_x(sp_, 7)
            with sp_.Fori(2, NPROJ) as t:
                for q in range(4):
                    load(q, 4 * t + q, w_in[bass.ds(t, 1), :, q * T:(q + 1) * T].rearrange("a p n -> (a p) n"), T)
            with sp_.Fori(0, KT) as t:
                for q in range(4):
                    load(q, 4 * t + (QN_OUT + q), w_out[bass.ds(t, 1), :, q * T:(q + 1) * T].rearrange("a p n -> (a p) n"), T)
            with sp_.Fori(0, FCH) as c:
                with sp_.Fori(0, 2 * FPC) as f:
                    for q in range(4):
                        load(q, QN_CHUNK * c + 4 * f + (QN_FFN + q),
                             w_gu[bass.ds(2 * FPC * c + f, 1), :, q * T:(q + 1) * T].rearrange("a p n -> (a p) n"), T)
                with sp_.Fori(0, KT) as d:
                    for q, (k0, kn) in enumerate(DOWN_K):
                        load(q, QN_CHUNK * c + 4 * d + (QN_FFN + 8 * FPC + q),
                             w_dn[bass.ds(KT * c + d, 1), :, k0 * P:(k0 + kn) * P].rearrange("a p n -> (a p) n"), kn * P)

        @block.gpsimd
        def _(pool):
            def low(slot, n, width):
                pool.wait_ge(hi_ready, n + 1)
                nc.gpsimd.tensor_tensor(wlo[:, slot % NW, 0:width], raw[:, slot % NRAW, 0:width],
                                        whi[:, slot % NW, 0:width].bitcast(F32), ALU.subtract).then_inc(lo_ready, 1)

            with pool.Fori(0, (QN_OUT - 4) // 8) as i:
                for q in range(8):
                    low(q, 8 * i + q, T)
            for q in range(QN_OUT - 4, QN_OUT):
                low(q, q, T)
            with pool.Fori(0, KT // 2) as i:
                for q in range(8):
                    low(QN_OUT + q, 8 * i + (QN_OUT + q), T)
            with pool.Fori(0, FCH) as c:
                with pool.Fori(0, FPC) as f:
                    for q in range(8):
                        low(QN_FFN + q, QN_CHUNK * c + 8 * f + (QN_FFN + q), T)
                with pool.Fori(0, KT // 2) as d:
                    for q in range(8):
                        low(QN_FFN + q, QN_CHUNK * c + 8 * d + (QN_FFN + 8 * FPC + q), DOWN_K[q % 4][1] * P)

        @block.tensor
        def _(pe):
            def quarter(slot, n, dst, src_hi, src_lo, ks, first, last, before=None):
                pe.wait_ge(lo_ready, n + 1)
                for i, k in enumerate(ks):
                    if before is not None:
                        before(k)
                    w = slice(i * P, (i + 1) * P)
                    s = slot % NW
                    nc.tensor.matmul(dst, whi[:, s, w], src_hi[:, k, :], start=first and i == 0, stop=False)
                    nc.tensor.matmul(dst, wlo[:, s, w], src_hi[:, k, :], start=False, stop=False)
                    ins = nc.tensor.matmul(dst, whi[:, s, w], src_lo[:, k, :], start=False,
                                           stop=last and i == len(ks) - 1)
                ins.then_inc(w_used, 1)

            def side(t, q):
                a = 4 * t + q
                kind, j, _ = TILES[t - 1] if 0 < t <= NPROJ else ("", 0, 0)
                if (t, q) == (1, 0):
                    pe.wait_ge(const_loaded, 16 * 3)
                    nc.tensor.matmul(ps[0:HEADS, 4, 0:384], relt, oneh_t[:, 0:384], start=True, stop=True)
                    nc.tensor.matmul(ps[:, 5, 0:HEADS], oneh_t[:, 384:512], relt, start=True, stop=True).then_inc(rows_ready, 1)
                if (t, q) == (2, XSUM_Q):
                    pe.wait_ge(x_acc, KT - 1)
                    nc.tensor.matmul(bank(2), C("ones"), sqsum[:, :], start=True, stop=True).then_inc(x_sum, 1)
                if (t, q) == (3, 1):
                    wait_read(pe, 0)
                    for c in range(NCH):
                        ins = nc.tensor.transpose(ps[:, 3, c * P:(c + 1) * P], misc[:, c * P:(c + 1) * P], C("ident"))
                    ins.then_inc(misc_tok, 1)
                if (t, q) == (4, 3):
                    pe.wait_ge(dt_ready, 1)
                    pe.wait_ge(misc_used, 1)
                    nc.tensor.matmul(ps[0:64, 3, 0:P], dta, C("triu"), start=True, stop=True)
                    nc.tensor.matmul(ps[:, 3, P:P + 64], C("triu"), dta, start=True, stop=True)
                    nc.tensor.matmul(ps[:, 3, P + 64:P + 128], C("ones"), dta, start=True, stop=True).then_inc(acs_sum, 1)
                if kind in ("q", "k") and q == 2:
                    m = j + (4 if kind == "k" else 0)
                    pe.wait_ge(nq_sq, m + 1)
                    if m >= 2:
                        pe.wait_ge(nq_done, m - 1)
                    nc.tensor.matmul(bank(4 + m % 2), C("halves"), nsq[:, m % 2, :], start=True, stop=True).then_inc(nq_sum, 1)
                if kind == "v" and q == 1:
                    wait_read(pe, t - 1)
                    if j >= 2:
                        pe.wait_ge(v_tok, j - 1)
                    for c in range(NCH):
                        ins = nc.tensor.transpose(ps[:, 6 + j % 2, c * P:(c + 1) * P], vT[:, j % 2, c * P:(c + 1) * P], C("ident"))
                    ins.then_inc(v_tr, 1)
                if IDX_AT <= a < IDX_AT + N_IDX // 2:
                    for e in (2 * (a - IDX_AT), 2 * (a - IDX_AT) + 1):
                        b, h = 1 + e // HEADS, e % HEADS
                        if e == 0:
                            wait_read(pe, TILE_OF["qi", 3])
                            wait_read(pe, TILE_OF["qi", 2])
                            pe.wait_ge(ki_dup, 16)
                            pe.wait_ge(acs_copied, 2)
                            pe.wait_ge(acs_diff, 1)
                        if e >= 2:
                            pe.wait_ge(idx_relu, e - 1)
                        rows = slice(64 * (h % 2), 64 * (h % 2) + 64)
                        key = misc if h % 2 == 0 else ki_hi
                        nc.tensor.matmul(ps[:, 2 + e % 2, 0:P * (b + 1)], qi[rows, h // 2, b * P:(b + 1) * P],
                                         key[rows, 0:P * (b + 1)], start=True, stop=True).then_inc(idx_s, 1)
                if ATT_AT <= a < ATT_AT + N_ATT + 3:
                    u = a - ATT_AT - 2
                    if 0 <= u < N_ATT:
                        b = u % NCH
                        pe.wait_ge(att_p, u + 1)
                        if u >= 2:
                            pe.wait_ge(att_pt, u - 1)
                        for kb in range(b + 1):
                            ins = nc.tensor.transpose(ps[:, 4 + u % 2, kb * P:(kb + 1) * P],
                                                      logit[:, u % 4, kb * P:(kb + 1) * P], C("ident"))
                        ins.then_inc(att_t, 1)
                    u = a - ATT_AT - 3
                    if 0 <= u < N_ATT:
                        h, b = u // NCH, u % NCH
                        pe.wait_ge(att_pt, u + 1)
                        if u == 0:
                            pe.wait_ge(v_tok, 4)
                        if h >= 4 and h % 2 == 0 and b == 0:
                            pe.wait_ge(att_out, h // 2 - 1)
                        for kb in range(b + 1):
                            ins = nc.tensor.matmul(ps[64 * (h % 2):64 * (h % 2) + 64, 6 + (h // 2) % 2, b * P:(b + 1) * P],
                                                   vtok[:, kb, h * 64:(h + 1) * 64], pT[:, u % 2, kb * P:(kb + 1) * P],
                                                   start=kb == 0, stop=kb == b)
                        ins.then_inc(att_pv, 1)
                    u = a - ATT_AT
                    if u < N_ATT:
                        h, b = u // NCH, u % NCH
                        if u == 0:
                            pe.wait_ge(nq_done, 8)
                        if u >= 2:
                            pe.wait_ge(att_log, u - 1)
                        rows = slice(64 * (h % 2), 64 * (h % 2) + 64)
                        nc.tensor.matmul(ps[:, 2 + u % 2, 0:P * (b + 1)], qkT[rows, h // 2, b * P:(b + 1) * P],
                                         qkT[rows, 4 + h // 2, 0:P * (b + 1)], start=True, stop=True).then_inc(att_s, 1)
                if (t, q) == (27, 3):
                    pe.wait_ge(conv_silu, 4)
                    pe.wait_ge(att_out, 4)
                    for g in range(2):
                        for c in range(NCH):
                            nc.tensor.transpose(ps[:, 6 + g, c * P:(c + 1) * P], bT[:, g, c * P:(c + 1) * P], C("ident"))
                        for c in range(NCH):
                            ins = nc.tensor.matmul(ps[:, 2 + g, c * P:(c + 1) * P], bT[:, g, c * P:(c + 1) * P],
                                                   cT[:, g, c * P:(c + 1) * P], start=True, stop=True)
                    ins.then_inc(bc_prep, 1)
                if t >= 28:
                    if (t - 29) % 2 == 0 and 0 <= (t - 29) // 2 < 8 and q == 2:
                        j2 = (t - 29) // 2
                        pe.wait_ge(conv_silu, 5 + j2)
                        pe.wait_ge(hst_ready, j2) if j2 else pe.wait_ge(bc_done, 1)
                        for c in range(NCH):
                            ins = nc.tensor.transpose(ps[:, 6, c * P:(c + 1) * P], xsT[:, c * P:(c + 1) * P], C("ident"))
                        ins.then_inc(xs_tr, 1)
                    if (t - 29) % 2 == 0 and 0 <= (t - 29) // 2 < 8 and q == 3:
                        j2 = (t - 29) // 2
                        pe.wait_ge(xdt_ready, j2 + 1)
                        for c in range(NCH - 1):
                            ins = nc.tensor.matmul(ps[:, 6, c * P:(c + 1) * P], btok[:, j2 // 4, c, :],
                                                   xdd[:, c, :, :].rearrange("p h d -> p (h d)"), start=True, stop=True)
                        ins.then_inc(st_ready, 1)
                    if (t - 30) % 2 == 0 and 0 <= (t - 30) // 2 < 8 and q == 0:
                        j2 = (t - 30) // 2
                        pe.wait_ge(hst_ready, j2 + 1)
                        pe.wait_ge(g_ready, j2 + 1)
                        if j2 >= 1:
                            pe.wait_ge(y_done, j2)
                        if j2 == 4:
                            pe.wait_ge(gn_done, 1)
                        for c in range(NCH):
                            for hh in range(2):
                                nc.tensor.matmul(ps[64 * hh:64 * hh + 64, 7, c * P:(c + 1) * P], xdt[:, c, hh, :],
                                                 gmat[:, hh, c, :], start=True, stop=c == 0)
                            for hh in range(2 if c else 0):
                                ins = nc.tensor.matmul(ps[64 * hh:64 * hh + 64, 7, c * P:(c + 1) * P], hst[:, c - 1, hh, :],
                                                       ce[:, hh, c - 1, :], start=False, stop=True)
                        ins.then_inc(y_ready, 1)
                    if (t, q) in ((36, 3), (44, 3)):
                        pe.wait_ge(y_done, 4 if t == 36 else 8)
                        nc.tensor.matmul(bank(7), C("ones"), gsum, start=True, stop=True).then_inc(gn_sum, 1)

            pe.wait_ge(zeros_ready, 1)
            for _ in range(WARM):
                nc.tensor.matmul(bank(5), zeros[:, 0:P], zeros, start=True, stop=True)

            for n in range(8):
                if n >= 4:
                    side(1, n - 4)
                quarter(n, n, acc(n % 2), hhi, hlo, range(4 * (n // 2), 4 * (n // 2) + 4), n < 2, n >= 6,
                        (lambda k: pe.wait_ge(h_lo, k + 1)) if n % 2 == 0 else None)
            for t in range(2, NPROJ):
                for q in range(4):
                    side(t, q)
                    if q == 0 and t >= 4:
                        wait_read(pe, t - 2)
                    quarter(4 * t + q, 4 * t + q, acc(t), hhi, hlo, range(4 * q, 4 * q + 4), q == 0, q == 3)

            for c in range(2):
                wait_read(pe, TN_OUT + c - 2)
                for q in range(4):
                    n = QN_OUT + 4 * c + q
                    quarter(n, n, bank((TN_OUT + c) % 2), yhi, ylo, range(4 * q, 4 * q + 4), q == 0, q == 3,
                            (lambda k: pe.wait_ge(y_lo, k + 1)) if c == 0 else None)
            with pe.Fori(1, KT // 2) as i:
                for c in range(2):
                    pe.wait_ge(acc_read[(TN_OUT + c) % 2], i + (TN_OUT + c - 2) // 2 + 1)
                    for q in range(4):
                        quarter(QN_OUT + 4 * c + q, 8 * i + (QN_OUT + 4 * c + q), bank((TN_OUT + c) % 2), yhi, ylo,
                                range(4 * q, 4 * q + 4), q == 0, q == 3)

            def gate_or_up(c, e, read):
                pe.wait_ge(acc_read[(TN_FFN + c) % 2], read + (TN_FFN + c - 2) // 2 + 1)
                for q in range(4):
                    if isinstance(e, int):
                        pe.wait_ge(h2_lo, KT if q == 3 else KT - 4)
                    quarter(QN_FFN + 4 * c + q, e + (QN_FFN + 4 * c + q), bank((TN_FFN + c) % 2),
                            hhi, hlo, range(4 * q, 4 * q + 4), q == 0, q == 3)

            gate_or_up(0, 0, 0)
            pe.wait_ge(x2_sum, KT + 1)
            nc.tensor.matmul(bank(4), C("ones"), sqsum[:, :], start=True, stop=True).then_inc(r2_sum, 1)
            gate_or_up(1, 0, 0)

            def down(ch):
                with pe.Fori(0, KT // 2) as d:
                    for c in range(2):
                        pe.wait_ge(acc_read[(TN_FFN + c) % 2],
                                   (TN_CHUNK // 2) * ch + d + (TN_FFN + 2 * FPC + c - 2) // 2 + 1)
                        for q, (k0, kn) in enumerate(DOWN_K):
                            pe.wait_ge(a_lo, FPC * ch + (FPC if q == 3 else FPC - 1))
                            n = QN_FFN + 8 * FPC + 4 * c + q
                            quarter(n, QN_CHUNK * ch + 8 * d + n, bank((TN_FFN + c) % 2), ahi, alo,
                                    range(k0, k0 + kn), q == 0, q == 3)

            with pe.Fori(1, FPC) as f:
                for c in range(2):
                    gate_or_up(c, 8 * f, f)
            down(0)
            with pe.Fori(1, FCH) as ch:
                with pe.Fori(0, FPC) as f:
                    for c in range(2):
                        gate_or_up(c, QN_CHUNK * ch + 8 * f, (TN_CHUNK // 2) * ch + f)
                down(ch)

        @block.scalar
        def _(sc):
            ch_ = Chain(sc, act_step)
            A = nc.scalar.activation

            def high(slot, n, loads, width=T):
                sc.wait_ge(raw_loaded[slot % NRAW], 16 * loads)
                if not isinstance(n, int) or n >= NW:
                    sc.wait_ge(w_used, n - NW + 1)
                A(whi[:, slot % NW, 0:width], raw[:, slot % NRAW, 0:width], ACT.Copy).then_inc(hi_ready, 1)

            def rsqrt(dst, src, scale, done):
                nc.scalar.preload_act_table_set("natural_log_exp_and_others")
                ch_.link(A(dst, src, ACT.Ln, bias=par("eps"), scale=scale))
                A(dst, dst, ACT.Exp, scale=-0.5).then_inc(done, 1)

            def side(t, q):
                a = 4 * t + q
                kind, j, _ = TILES[t - 1] if 0 < t <= NPROJ else ("", 0, 0)
                if kind in ("q", "k") and q == 0:
                    m = j + (4 if kind == "k" else 0)
                    wait_read(sc, t - 1)
                    if m >= 2:
                        sc.wait_ge(nq_sum, m - 1)
                    A(nsq[:, m % 2, :], qkT[:, m, :], ACT.Square).then_inc(nq_sq, 1)
                if kind == "z" and q == 0:
                    wait_read(sc, t - 1)
                    A(zs[:, j % 2, :], zs[:, j % 2, :], ACT.Silu).then_inc(z_silu, 1)
                if kind == "conv" and q == (2 if j < 4 else 1):
                    sc.wait_ge(conv_done, j + 1)
                    if j > 4:
                        sc.wait_ge(y_done, j - 4)
                    dst = bT[:, j, :] if j < 2 else cT[:, j - 2, :] if j < 4 else xsT
                    ci = 8 + j if j < 4 else j - 4
                    A(dst, cacc, ACT.Silu, bias=par("cb", ci)).then_inc(conv_silu, 1)
                if (t, q) == (2, XSUM_Q):
                    sc.wait_ge(x_sum, 1)
                    rsqrt(sqsum[:, :], bank(2), 1.0 / D, x_r0)
                if (t, q) == (1, 0):
                    sc.wait_ge(rows_ready, 1)
                    A(rrow, ps[0:HEADS, 4, 0:384], ACT.Copy).then_inc(rows_copied, 1)
                    A(far, ps[:, 5, 0:HEADS], ACT.Copy).then_inc(rows_copied, 1)
                if (t, q) == (3, 1):
                    wait_read(sc, 0)
                    sc.dma_start(ki_hi[64:128, :], misc[0:64, :]).then_inc(ki_dup, 16)
                    sc.wait_ge(rows_copied, 2)
                    sc.dma_start(bias_rows.rearrange("r h x -> h r x"),
                                 rrow.unsqueeze(1).to_broadcast([HEADS, P, 384])).then_inc(rows_stored, 16)
                if (t, q) == (3, 3):
                    sc.wait_ge(sp_in, 1)
                    A(sp[1], sp[0], ACT.Exp).then_inc(sp_exp, 1)
                    A(ealog, par("alog", 0, 16), ACT.Exp).then_inc(sp_exp, 1)
                if (t, q) == (5, 0):
                    sc.wait_ge(acs_diff, 1)
                    A(acs_row, ps[0:64, 3, 0:P], ACT.Copy).then_inc(acs_copied, 1)
                    A(total, ps[:, 3, P + 64:P + 128], ACT.Exp).then_inc(acs_copied, 1)
                    sc.wait_ge(acs_copied, 2)
                    sc.dma_start(acs_rows.rearrange("h c l -> (h c) l"), acs_row).then_inc(acs_stored, 16)
                if (t, q) == (5, 0):
                    sc.wait_ge(acs_diff, 1)
                    A(to_end, to_end, ACT.Exp).then_inc(acs_exp, 1)
                if (t, q) == (27, 0) or (t >= 29 and (t - 29) % 2 == 0 and (t - 29) // 2 < 7 and q == 0):
                    j2 = (t - 27) // 2
                    if j2 == 0:
                        sc.wait_ge(acs_stored, 16)
                    else:
                        sc.wait_ge(seg_ready, j2)
                        sc.wait_ge(lt_ready, j2)
                    sc.dma_start(rows.rearrange("p h c l -> p (h c l)"),
                                 acs_rows[2 * j2:2 * j2 + 2].rearrange("(a h) c l -> a (h c l)", a=1).to_broadcast([P, 8 * P])
                                 ).then_inc(rows_loaded, 16)
                if (t, q) == (4, 0):
                    sc.wait_ge(rows_stored, 16)
                    sc.wait_ge(h_lo, KT)
                    sc.dma_start(btile, bass.AP(bias_rows.tensor, P - 1, [[HEADS * 384 - 1, P], [384, HEADS], [1, 2 * P]])
                                 ).then_inc(btile_loaded, 16)
                if kind in ("q", "k") and q == 3:
                    m = j + (4 if kind == "k" else 0)
                    sc.wait_ge(nq_sum, m + 1)
                    if m:
                        sc.wait_ge(nq_done, m)
                    rsqrt(nrs, bank(4 + m % 2), 1.0 / 64, nq_r0)
                if IDX_AT <= a < IDX_AT + N_IDX // 2:
                    for e in (2 * (a - IDX_AT), 2 * (a - IDX_AT) + 1):
                        b = 1 + e // HEADS
                        sc.wait_ge(idx_s, e + 1)
                        if e >= 2:
                            sc.wait_ge(idx_acc, e - 1)
                        A(relu[:, e % 2, 0:P * (b + 1)], ps[:, 2 + e % 2, 0:P * (b + 1)], ACT.Relu).then_inc(idx_relu, 1)
                if ATT_AT <= a < ATT_AT + N_ATT + 3:
                    u = a - ATT_AT - 2
                    if 0 <= u < N_ATT:
                        b = u % NCH
                        sc.wait_ge(att_t, u + 1)
                        if u >= 2:
                            sc.wait_ge(att_pv, u - 1)
                        A(pT[:, u % 2, 0:P * (b + 1)], ps[:, 4 + u % 2, 0:P * (b + 1)], ACT.Copy).then_inc(att_pt, 1)
                    u = a - ATT_AT
                    if u < N_ATT:
                        b = u % NCH
                        sc.wait_ge(att_max, u + 1)
                        x = logit[:, u % 4, 0:P * (b + 1)]
                        A(x, x, ACT.Exp, bias=nmax[:, u % 4:u % 4 + 1], accum_out=rsum[:, u % 4:u % 4 + 1]).then_inc(att_exp, 1)
                    u = a - ATT_AT - 3
                    if 0 <= u < N_ATT and u % 8 == 7:
                        sc.wait_ge(att_pv, u + 1)
                        A(resid[:, 8 + u // 8, :], bank(6 + (u // 8) % 2), ACT.Copy).then_inc(att_out, 1)
                if t >= 28 and (t - 28) % 2 == 0 and (t - 28) // 2 < 8 and q == 2:
                    j2 = (t - 28) // 2
                    sc.wait_ge(rows_loaded, 16 * (j2 + 1))
                    if j2:
                        sc.wait_ge(y_ready, j2)
                    A(ce.rearrange("p h c l -> p h (c l)"), rows[:, :, 1:4, :].rearrange("p h c l -> p h (c l)"), ACT.Exp)
                    sc.wait_ge(seg_ready, j2 + 1)
                    g1 = gmat.rearrange("p h c l -> p (h c l)")
                    A(g1, g1, ACT.Exp).then_inc(lt_ready, 1)
                if (t, q) in ((36, 3), (44, 3)):
                    sc.wait_ge(gn_sum, 1 if t == 36 else 2)
                    rsqrt(nrs, bank(7), 1.0 / 512, gn_r0)
                if SPLIT_AT <= a < SPLIT_AT + 16:
                    split_high(a - SPLIT_AT)
                if (t, q) == (48, 3):
                    for i in range(6):
                        reload(i)

            def split_high(k):
                if k == 0:
                    sc.wait_ge(gn_done, 8)
                    sc.wait_ge(sc_done, 3)
                if k == 15:
                    sc.wait_ge(sc_done, 4)
                A(yhi[:, k, :], resid[:, k, :], ACT.Copy).then_inc(y_hi, 1)

            def reload(i):
                sc.wait_ge(y_lo, 2 * i + 2)
                load_x(sc, i)

            sc.dma_start(pc[:, :], params).then_inc(par_loaded, 16)
            nc.scalar.preload_act_table_set("natural_log_exp_and_others")
            sc.wait_ge(par_loaded, 16)
            def square(k):
                if k >= 3:
                    sc.wait_ge(x_acc, k - 2)
                A(nsq[:, k % 2, :] if k else sqsum[:, :], resid[:, k, :], ACT.Square).then_inc(x_sq, 1)

            for k in range(KT):
                if k % 2 == 0:
                    high(k // 2, k // 2, k // 8 + 1)
                    sc.wait_ge(x_loaded[k // 2], 16)
                A(hhi[:, k, :], resid[:, k, :], ACT.Copy, scale=par("gmix", k)).then_inc(h_hi, 1)
                if k >= SQ_LAG:
                    square(k - SQ_LAG)
                if k == 7:
                    sc.dma_start(oneh_t, onehot).then_inc(const_loaded, 16)
                    sc.dma_start(relt, relb).then_inc(const_loaded, 16)
                    sc.dma_start(cm[:, :, :], cmats).then_inc(const_loaded, 16)
            for k in range(KT - SQ_LAG, KT):
                square(k)

            for t in range(2, NPROJ + 2):
                for q in range(4):
                    high(4 * t + q, 4 * t + q, t + 1)
                    side(t - 1, q)

            reload(6)
            reload(7)

            def residual(d, n):
                sc.wait_ge(acc_read[(TN_OUT + n[1]) % 2], n[2])
                sc.wait_ge(x2_sum, n[0])
                A(bank(2 + n[1]), resid_block(d), ACT.Square).then_inc(x2_sq, 1)
                A(hhi_block(d), resid_block(d), ACT.Copy, scale=pc[:, bass.ds(d + PC["gffn"], 1)]).then_inc(h2_hi, 1)

            def resid_block(d):
                return resid[:, bass.ds(d, 1), :].rearrange("p a t -> p (a t)")

            def hhi_block(d):
                return hhi[:, bass.ds(d, 1), :].rearrange("p a t -> p (a t)")

            def highs(q0, n0, e, coef, width=(T,) * 4):
                for q in range(q0, q0 + 4):
                    n = n0 + q
                    high(n, e + n, coef + (n // 4 + 1), width[q % 4])

            with sc.Fori(1, KT // 2) as i:
                highs(0, QN_OUT, 8 * i, 2 * i)
                residual(2 * i - 2, (2 * i - 1, 0, i + TN_OUT // 2))
                highs(4, QN_OUT, 8 * i, 2 * i)
                residual(2 * i - 1, (2 * i, 1, i + (TN_OUT + 1) // 2))

            DW = [kn * P for _, kn in DOWN_K]

            def silu(n):
                sc.wait_ge(f_conv, n)
                A(gsilu[:, :], gconv[:, :], ACT.Silu).then_inc(f_silu, 1)

            def act_high(f, n):
                sc.wait_ge(f_act, n)
                A(ahi[:, bass.ds(f, 1), :].rearrange("p a t -> p (a t)"), act[:, :], ACT.Copy).then_inc(a_hi, 1)

            def mlp_chunk(c, first=False, last=False):
                e0, c0 = QN_CHUNK * c, (QN_CHUNK // 4) * c
                highs(0, QN_FFN, e0, c0)
                if first:
                    residual(KT - 2, (KT - 1, 0, KT // 2 + TN_OUT // 2))
                highs(4, QN_FFN, e0, c0)
                if first:
                    residual(KT - 1, (KT, 1, KT // 2 + (TN_OUT + 1) // 2))
                    sc.wait_ge(r2_sum, 1)
                    rsqrt(rstd2[:, :], bank(4), 1.0 / D, r2_r0)
                with sc.Fori(1, FPC) as f:
                    highs(0, QN_FFN, e0 + 8 * f, c0 + 2 * f)
                    silu(FPC * c + f)
                    highs(4, QN_FFN, e0 + 8 * f, c0 + 2 * f)
                    act_high(f - 1, FPC * c + f)
                q0 = QN_FFN + 8 * FPC
                highs(0, q0, e0, c0, DW)
                silu(FPC * c + FPC)
                highs(4, q0, e0, c0, DW)
                act_high(FPC - 1, FPC * c + FPC)
                with sc.Fori(1, KT // 2) as d:
                    highs(0, q0, e0 + 8 * d, c0 + 2 * d, DW)
                    if last:
                        store(2 * d - 2, 0, d)
                    highs(4, q0, e0 + 8 * d, c0 + 2 * d, DW)
                    if last:
                        store(2 * d - 1, 1, d)

            def store(d, parity, n):
                t0 = TN_FFN + TN_CHUNK * (FCH - 1) + 2 * FPC + parity
                sc.wait_ge(acc_read[t0 % 2], t0 // 2 + n)
                sc.dma_start(out[bass.ds(d, 1), :, :].rearrange("a p t -> (a p) t"), resid_block(d)).then_inc(out_stored, 16)

            mlp_chunk(0, first=True)
            with sc.Fori(1, FCH - 1) as c:
                mlp_chunk(c)
            mlp_chunk(FCH - 1, last=True)
            store(KT - 2, 0, KT // 2)
            store(KT - 1, 1, KT // 2)
            sc.wait_ge(out_stored, 16 * KT)

        @block.vector
        def _(ve):
            V = nc.vector
            ch_ = Chain(ve, vec)
            rounds_of = topk_rounds()

            def newton(r, t, total, n):
                ch_.link(V.scalar_tensor_tensor(t, total, EPS * n, r, ALU.add, ALU.mult))
                ch_.link(V.scalar_tensor_tensor(t, t, -0.5 / n, r, ALU.mult, ALU.mult))
                ch_.link(V.scalar_tensor_tensor(r, t, 1.5, r, ALU.add, ALU.mult))

            def read_out(t):
                kind, j, _ = TILES[t]
                m = j + (4 if kind == "k" else 0)
                wait_tile(ve, t)
                if kind == "q" and j == 0:
                    ve.wait_ge(dt_ready, 1)
                if kind == "v" and j >= 2:
                    ve.wait_ge(v_tr, j - 1)
                if kind in ("scb", "scc", "sch") and j:
                    ve.wait_ge(sc_done, j)
                if kind == "conv" and j:
                    ve.wait_ge(conv_done, j)
                if kind == "z" and j >= 2:
                    ve.wait_ge(y_done, j - 1)
                dst = {"misc": lambda: misc, "qi": lambda: qi[:, j, :], "q": lambda: qkT[:, m, :], "k": lambda: qkT[:, m, :],
                       "v": lambda: vT[:, j % 2, :], "scb": lambda: scb, "scc": lambda: scm[:, 2:], "sch": lambda: scm[:, 2:],
                       "conv": lambda: cpad[:, 3:], "z": lambda: zs[:, j % 2, :]}[kind]()
                if kind == "sch":
                    wait_read(ve, t - 1)
                    V.tensor_tensor(dst, acc(t), dst, ALU.mult).then_inc(acc_read[t % 2], 1)
                    wait_read(ve, t)
                    ch_.link(V.tensor_tensor(dst, dst, sqsum[:, :], ALU.mult))
                else:
                    V.tensor_tensor(dst, acc(t), sqsum[:, :], ALU.mult).then_inc(acc_read[t % 2], 1)

            def side(t, q):
                a = 4 * t + q
                kind, j, _ = TILES[t - 1] if 0 < t <= NPROJ else ("", 0, 0)
                if (t, q) == (2, XSUM_Q):
                    ve.wait_ge(x_r0, 1)
                    newton(sqsum[:, :], ntmp, bank(2), D)
                    read_out(0)
                    read_out(1)
                attending = ATT_AT <= a < ATT_AT + N_ATT + 3
                if q == 0 and t >= 3 and kind and not attending:
                    read_out(t - 1)
                if (t, q) == (3, 2):
                    ve.wait_ge(misc_tok, 1)
                    m3 = bank(3).rearrange("p (c n) -> p c n", c=4)
                    V.tensor_copy(widx, m3[:, :, M_WI:M_WI + HEADS])
                    V.tensor_tensor(sp[2], m3[:, :, M_DT:M_DT + SSD_HEADS],
                                    par("dtb", 0, 16).unsqueeze(1).to_broadcast([P, 4, SSD_HEADS]), ALU.add).then_inc(misc_used, 1)
                    ve.wait_ge(misc_used, 1)
                    V.scalar_tensor_tensor(sp[0], sp[2], -1.0, sp[2], ALU.mult, ALU.min).then_inc(sp_in, 1)
                if (t, q) == (4, 0):
                    ve.wait_ge(sp_exp, 2)
                    u, x, den, z2, p = sp[1], sp[2], sp[3], sp[4], sp[5]
                    ch_.link(V.tensor_scalar(den, u, 2.0, None, ALU.add))
                    ch_.link(V.reciprocal(den, den))
                    ch_.link(V.tensor_tensor(u, u, den, ALU.mult))
                    ch_.link(V.tensor_tensor(z2, u, u, ALU.mult))
                    ch_.link(V.tensor_scalar(p, z2, LOG1P[8], None, ALU.mult))
                    for i in range(7, 0, -1):
                        ch_.link(V.scalar_tensor_tensor(p, p, LOG1P[i], z2, ALU.add, ALU.mult))
                    ch_.link(V.scalar_tensor_tensor(p, p, 1.0, u, ALU.add, ALU.mult))
                    ch_.link(V.tensor_scalar(x, x, 0.0, None, ALU.max))
                    ch_.link(V.scalar_tensor_tensor(dt, p, 2.0, x, ALU.mult, ALU.add))
                    V.scalar_tensor_tensor(dta.rearrange("p (h c) -> p c h", h=SSD_HEADS), dt, -1.0, ealog.unsqueeze(1).to_broadcast([P, 4, SSD_HEADS]),
                                           ALU.mult, ALU.mult).then_inc(dt_ready, 1)
                if (t, q) == (5, 0):
                    ve.wait_ge(acs_sum, 1)
                    ch_.link(V.tensor_copy(acs, ps[:, 3, P:P + 64]))
                    V.tensor_tensor(to_end, ps[:, 3, P + 64:P + 128], acs, ALU.subtract).then_inc(acs_diff, 1)
                kind2, j2 = TILES[t - 2][:2] if 2 <= t <= NPROJ + 1 else ("", 0)
                if kind2 in ("q", "k") and q == 1:
                    m = j2 + (4 if kind2 == "k" else 0)
                    ve.wait_ge(nq_r0, m + 1)
                    newton(nrs, ntmp, bank(4 + m % 2), 64)
                    wait_read(ve, t - 2)
                    V.scalar_tensor_tensor(qkT[:, m, :], qkT[:, m, :], par("g" + kind2), nrs, ALU.mult, ALU.mult).then_inc(nq_done, 1)
                if kind == "v" and q == 2:
                    ve.wait_ge(v_tr, j + 1)
                    V.tensor_copy(vtok[:, :, j * P:(j + 1) * P], bank(6 + j % 2).rearrange("p (c d) -> p c d", c=4)).then_inc(v_tok, 1)
                if IDX_AT <= a < IDX_AT + N_IDX // 2:
                    for e in (2 * (a - IDX_AT), 2 * (a - IDX_AT) + 1):
                        b, h = 1 + e // HEADS, e % HEADS
                        ve.wait_ge(idx_relu, e + 1)
                        r = relu[:, e % 2, 0:P * (b + 1)]
                        if h == 0:
                            V.tensor_scalar(score[b], r, widx[:, b, h:h + 1], None, ALU.mult).then_inc(idx_acc, 1)
                        else:
                            ve.wait_ge(idx_acc, e)
                            V.scalar_tensor_tensor(score[b], r, widx[:, b, h:h + 1], score[b], ALU.mult, ALU.add).then_inc(idx_acc, 1)
                        if h == HEADS - 1:
                            ve.wait_ge(idx_acc, e + 1)
                            ch_.link(V.tensor_tensor(score[b][:, b * P:], score[b][:, b * P:], C("causal"), ALU.add))
                if a in rounds_of:
                    for r in rounds_of[a]:
                        b, last = 1 + r // (TOPK // 8), r % (TOPK // 8) == TOPK // 8 - 1
                        ch_.link(V.max(top8, score[b]))
                        ch_.link(V.match_replace(score[b], top8, score[b], TAKEN))
                        if last:
                            V.tensor_scalar(score[b], score[b], 0.5 * TAKEN, NEG, ALU.is_gt, ALU.mult).then_inc(mask_ready, 1)
                if attending:
                    u = a - ATT_AT - 1
                    if 0 <= u < N_ATT:
                        b, s = u % NCH, slice(u % 4, u % 4 + 1)
                        ve.wait_ge(att_exp, u + 1)
                        ch_.link(V.reciprocal(rinv[:, s], rsum[:, s]))
                        x = logit[:, u % 4, 0:P * (b + 1)]
                        V.tensor_scalar(x, x, rinv[:, s], None, ALU.mult).then_inc(att_p, 1)
                    u = a - ATT_AT
                    if u < N_ATT:
                        h, b, s = u // NCH, u % NCH, slice(u % 4, u % 4 + 1)
                        if u == 0:
                            ve.wait_ge(btile_loaded, 16)
                            ve.wait_ge(acs_stored, 16)
                            ve.wait_ge(mask_ready, 3)
                        ve.wait_ge(att_s, u + 1)
                        if u >= 4:
                            ve.wait_ge(att_t, u - 3)
                        x, near = logit[:, u % 4, 0:P * (b + 1)], P * max(b - 1, 0)
                        if near:
                            V.tensor_scalar(x[:, 0:near], ps[:, 2 + u % 2, 0:near], 0.125, far[:, h:h + 1], ALU.mult, ALU.add)
                        V.scalar_tensor_tensor(x[:, near:], ps[:, 2 + u % 2, near:P * (b + 1)], 0.125,
                                               btile[:, h, (P if b == 0 else 0):2 * P], ALU.mult, ALU.add).then_inc(att_log, 1)
                        ve.wait_ge(att_log, u + 1)
                        ch_.link(V.tensor_tensor_reduce(out=x, in0=x, in1=C("causal") if b == 0 else score[b], scale=1.0,
                                                        scalar=TAKEN, op0=ALU.add, op1=ALU.max, accum_out=rmax[:, s]))
                        V.tensor_scalar(nmax[:, s], rmax[:, s], -1.0, None, ALU.mult).then_inc(att_max, 1)
                if q == 0 and attending:
                    read_out(t - 1)
                if kind == "sch" and q == (1 if j < 2 else 0):
                    ch_.link(V.tensor_scalar(scu, scm[:, 2:], par("scw", 3 * j + 2), None, ALU.mult))
                    ch_.link(V.scalar_tensor_tensor(scu, scm[:, 1:T + 1], par("scw", 3 * j + 1), scu, ALU.mult, ALU.add))
                    ch_.link(V.scalar_tensor_tensor(scu, scm[:, 0:T], par("scw", 3 * j), scu, ALU.mult, ALU.add))
                    V.tensor_tensor(resid[:, 12 + j, :], scu, scb, ALU.mult).then_inc(sc_done, 1)
                if kind == "conv" and q == 0:
                    wait_read(ve, t - 1)
                    if j:
                        ve.wait_ge(conv_silu, j)
                    ci = 8 + j if j < 4 else j - 4
                    ch_.link(V.tensor_scalar(cacc, cpad[:, 3:], par("cw", 4 * ci + 3), None, ALU.mult))
                    ch_.link(V.scalar_tensor_tensor(cacc, cpad[:, 2:2 + T], par("cw", 4 * ci + 2), cacc, ALU.mult, ALU.add))
                if kind == "conv" and q == (1 if j < 4 else 0):
                    ci = 8 + j if j < 4 else j - 4
                    ch_.link(V.scalar_tensor_tensor(cacc, cpad[:, 1:1 + T], par("cw", 4 * ci + 1), cacc, ALU.mult, ALU.add))
                    V.scalar_tensor_tensor(cacc, cpad[:, 0:T], par("cw", 4 * ci), cacc, ALU.mult, ALU.add).then_inc(conv_done, 1)
                if (t, q) == (28, 0):
                    ve.wait_ge(bc_prep, 1)
                    for g in range(2):
                        V.tensor_copy(btok[:, g, :, :].rearrange("p c n -> p (c n)"), bank(6 + g))
                        ins = V.tensor_tensor(cbt[:, g, :, :], bank(2 + g).rearrange("p (c l) -> p c l", c=4),
                                              C("triu").unsqueeze(1).to_broadcast([P, 4, P]), ALU.mult)
                    ins.then_inc(bc_done, 1)
                if t >= 28:
                    if (t - 28) % 2 == 0 and (t - 28) // 2 < 8:
                        j2 = (t - 28) // 2
                        g = j2 // 4
                        if q == 1:
                            ve.wait_ge(rows_loaded, 16 * (j2 + 1))
                            if j2:
                                ve.wait_ge(y_ready, j2)
                            acs_s = acs[:, 8 * j2:8 * j2 + 8].rearrange("p (h c) -> p h c", h=2).unsqueeze(3).to_broadcast([P, 2, 4, P])
                            ch_.link(V.tensor_tensor(gmat, rows, acs_s, ALU.min))
                            V.tensor_tensor(gmat, gmat, acs_s, ALU.subtract).then_inc(seg_ready, 1)
                        if q == 3:
                            ve.wait_ge(lt_ready, j2 + 1)
                            if j2 == 0:
                                ve.wait_ge(bc_done, 1)
                            V.tensor_tensor(gmat, gmat, cbt[:, g:g + 1, :, :].to_broadcast([P, 2, 4, P]), ALU.mult)
                            V.tensor_tensor(ce, ce, cT[:, g, P:T].rearrange("p (c l) -> p c l", c=3).unsqueeze(1).to_broadcast([P, 2, 3, P]),
                                            ALU.mult).then_inc(g_ready, 1)
                    if (t - 29) % 2 == 0 and 0 <= (t - 29) // 2 < 8:
                        j2 = (t - 29) // 2
                        if q == 2:
                            ve.wait_ge(xs_tr, j2 + 1)
                            ve.wait_ge(acs_exp, 1)
                            ch_.link(V.tensor_tensor(xdt, bank(6).rearrange("p (c h d) -> p c h d", c=4, h=2),
                                                     dt[:, :, 2 * j2:2 * j2 + 2].unsqueeze(3).to_broadcast([P, 4, 2, 64]), ALU.mult))
                            V.tensor_tensor(xdd, xdt[:, 0:3, :, :], to_end[:, 8 * j2:8 * j2 + 8].rearrange("p (h c) -> p c h", h=2)[:, 0:3, :]
                                            .unsqueeze(3).to_broadcast([P, 3, 2, 64]),
                                            ALU.mult).then_inc(xdt_ready, 1)
                        if q == 3:
                            ve.wait_ge(st_ready, j2 + 1)
                            b6 = bank(6).rearrange("p (c h d) -> p c h d", c=4, h=2)
                            ch_.link(V.tensor_copy(hst[:, 0, :, :], b6[:, 0, :, :]))
                            for c in (1, 2):
                                for hh in range(2):
                                    ins = V.scalar_tensor_tensor(hst[:, c, hh, :], hst[:, c - 1, hh, :], total[:, 4 * (2 * j2 + hh) + c:4 * (2 * j2 + hh) + c + 1],
                                                                 b6[:, c, hh, :], ALU.mult, ALU.add)
                                    if c == 1:
                                        ch_.link(ins)
                            ins.then_inc(hst_ready, 1)
                    if (t - 30) % 2 == 0 and 0 <= (t - 30) // 2 < 8 and q == 1:
                        j2 = (t - 30) // 2
                        y = resid[:, j2, :]
                        ve.wait_ge(y_ready, j2 + 1)
                        ch_.link(V.scalar_tensor_tensor(y, xsT, par("dskip", j2), bank(7), ALU.mult, ALU.add))
                        ve.wait_ge(z_silu, j2 + 1)
                        ch_.link(V.tensor_tensor(y, y, zs[:, j2 % 2, :], ALU.mult))
                        if j2 % 4 == 0:
                            V.tensor_tensor(gsum, y, y, ALU.mult).then_inc(y_done, 1)
                        else:
                            ch_.link(V.tensor_tensor(gtmp, y, y, ALU.mult))
                            V.tensor_tensor(gsum, gsum, gtmp, ALU.add).then_inc(y_done, 1)
                    if (t, q) in ((37, 0), (45, 0)):
                        g = 0 if t == 37 else 1
                        ve.wait_ge(gn_r0, g + 1)
                        newton(nrs, ntmp, bank(7), 512)
                    for j3 in {(37, 1): (0,), (38, 2): (1, 2, 3), (45, 1): (4, 5, 6, 7)}.get((t, q), ()):
                        V.scalar_tensor_tensor(resid[:, j3, :], resid[:, j3, :], par("gssd", j3), nrs,
                                               ALU.mult, ALU.mult).then_inc(gn_done, 1)
                if SPLIT_AT <= a < SPLIT_AT + 16:
                    k = a - SPLIT_AT
                    ve.wait_ge(y_hi, k + 1)
                    if k == 12:
                        ve.wait_ge(sc_done, 4)
                    V.tensor_tensor(ylo[:, k, :], resid[:, k, :], yhi[:, k, :].bitcast(F32), ALU.subtract).then_inc(y_lo, 1)

            V.memset(zeros, 0.0).then_inc(zeros_ready, 1)

            ve.wait_ge(par_loaded, 16)

            def add_square(k):
                ve.wait_ge(x_sq, k + 1)
                if k >= 2:
                    ve.wait_ge(x_acc, k - 1)
                V.tensor_tensor(sqsum[:, :], sqsum[:, :], nsq[:, k % 2, :], ALU.add).then_inc(x_acc, 1)

            for k in range(KT):
                ve.wait_ge(h_hi, k + 1)
                V.scalar_tensor_tensor(hlo[:, k, :], resid[:, k, :], par("gmix", k), hhi[:, k, :].bitcast(F32),
                                       ALU.mult, ALU.subtract).then_inc(h_lo, 1)
                if k > SQ_LAG:
                    add_square(k - SQ_LAG)
            for k in range(KT - SQ_LAG, KT):
                add_square(k)
            V.memset(scm[:, 0:2], 0.0)

            for t in range(NPROJ + 1):
                for q in range(4):
                    if (t, q) == (23, 0):
                        V.memset(cpad[:, 0:3], 0.0)
                    side(t, q)

            def blk(x, d):
                return x[:, bass.ds(d, 1), :].rearrange("p a t -> p (a t)")

            def residual(d, c, done, n):
                ve.wait_ge(w_used, done)
                V.tensor_tensor(blk(resid, d), bank((TN_OUT + c) % 2), blk(resid, d), ALU.add).then_inc(acc_read[(TN_OUT + c) % 2], 1)
                ve.wait_ge(x2_sq, n)
                ve.wait_ge(x2_sum, n)
                V.tensor_tensor(sqsum[:, :], sqsum[:, :], bank(2 + c), ALU.add).then_inc(x2_sum, 1)
                ve.wait_ge(h2_hi, n)
                V.scalar_tensor_tensor(blk(hlo, d), blk(resid, d), pc[:, bass.ds(d + PC["gffn"], 1)], blk(hhi, d).bitcast(F32),
                                       ALU.mult, ALU.subtract).then_inc(h2_lo, 1)

            V.memset(sqsum[:, :], 0.0).then_inc(x2_sum, 1)
            ve.wait_ge(x_loaded[0], 32)
            for c in range(2):
                residual(c, c, QN_OUT + 4 * c + 4, c + 1)
            for i in range(1, 8):
                ve.wait_ge(x_loaded[i], 32)
            with ve.Fori(1, KT // 2) as i:
                for c in range(2):
                    residual(2 * i + c, c, 8 * i + (QN_OUT + 4 * c + 4), 2 * i + (c + 1))

            ve.wait_ge(r2_r0, 1)
            newton(rstd2[:, :], ntmp2[:, :], bank(4), D)
            ch_.link(V.memset(gpad[:, 0:2], 0.0))
            links = ch_.n
            per_f = 2

            with ve.Fori(0, FCH) as c:
                with ve.Fori(0, FPC) as f:
                    ch_.n, ch_.base = 0, per_f * FPC * c + per_f * f + links
                    q0 = QN_CHUNK * c + 8 * f + QN_FFN
                    count = FPC * c + f
                    taps = [pc[:, bass.ds(3 * FPC * c + 3 * f + (PC["fcw"] + i), 1)] for i in range(3)]
                    ve.wait_ge(w_used, q0 + 4)
                    V.tensor_tensor(gpad[:, 2:], bank(TN_FFN % 2), rstd2[:, :], ALU.mult).then_inc(acc_read[TN_FFN % 2], 1)
                    ve.wait_ge(acc_read[TN_FFN % 2], (TN_CHUNK // 2) * c + f + (TN_FFN // 2 + 1))
                    ch_.link(V.tensor_scalar(gconv[:, :], gpad[:, 2:], taps[2], None, ALU.mult))
                    ch_.link(V.scalar_tensor_tensor(gconv[:, :], gpad[:, 1:T + 1], taps[1], gconv[:, :], ALU.mult, ALU.add))
                    V.scalar_tensor_tensor(gconv[:, :], gpad[:, 0:T], taps[0], gconv[:, :], ALU.mult, ALU.add).then_inc(f_conv, 1)
                    assert ch_.n == per_f
                    ve.wait_ge(w_used, q0 + 8)
                    par1 = (TN_FFN + 1) % 2
                    V.tensor_tensor(upv[:, :], bank(par1), rstd2[:, :], ALU.mult).then_inc(acc_read[par1], 1)
                    ve.wait_ge(acc_read[par1], (TN_CHUNK // 2) * c + f + ((TN_FFN + 1) // 2 + 1))
                    ve.wait_ge(f_silu, count + 1)
                    V.tensor_tensor(act[:, :], upv[:, :], gsilu[:, :], ALU.mult).then_inc(f_act, 1)
                    ve.wait_ge(f_act, count + 1)
                    ve.wait_ge(a_hi, count + 1)
                    V.tensor_tensor(blk(alo, f), act[:, :], blk(ahi, f).bitcast(F32), ALU.subtract).then_inc(a_lo, 1)
                with ve.Fori(0, KT // 2) as d:
                    for p in range(2):
                        ve.wait_ge(w_used, QN_CHUNK * c + 8 * d + (QN_FFN + 8 * FPC + 4 * p + 4))
                        V.tensor_tensor(blk(resid, 2 * d + p), bank((TN_FFN + p) % 2), blk(resid, 2 * d + p),
                                        ALU.add).then_inc(acc_read[(TN_FFN + p) % 2], 1)


def bucket_of(dist):
    n = np.maximum(dist, 0)
    exact = BUCKETS // 2
    large = exact + (np.log(np.maximum(n, exact).astype(np.float32) / np.float32(exact))
                     / np.float32(np.log(128 / exact)) * (BUCKETS - exact)).astype(np.int32)
    return np.where(n < exact, n, np.minimum(large, BUCKETS - 1))


def constants():
    i = np.arange(P)
    r, c = i[:, None], i[None, :]
    m = {"ident": r == c, "triu": r <= c, "causal": np.where(c > r, NEG, 0.0),
         "ones": np.ones((P, P)), "halves": (r // 64) == (c // 64)}
    cm = np.stack([np.asarray(m[n], np.float32) for n in CM_NAMES], axis=1)
    oh = np.zeros((BUCKETS, 512), np.float32)
    oh[bucket_of(255 - np.arange(384)), np.arange(384)] = 1.0
    oh[BUCKETS - 1, 384:] = 1.0
    return np.ascontiguousarray(cm), oh


def lay_out(x, norm_mix, w_in, ssd_conv_w, ssd_conv_b, ssd_dt_bias, ssd_a_log, ssd_d, ssd_norm, att_q_norm, att_k_norm,
            rel_bias, sc_conv_w, w_out, norm_ffn, ffn_w_gate, ffn_w_up, ffn_conv_w, ffn_w_down):
    f = np.float32
    a = {}
    a["xT"] = np.ascontiguousarray(x[0].T.reshape(KT, P, T).transpose(1, 0, 2))
    w = w_in[0]
    cols = []
    for kind, j, at in TILES:
        if kind == "misc":
            m = np.zeros((D, P), f)
            m[:, M_KI:M_KI + 64] = w[:, OFF_KI:OFF_KI + 64]
            m[:, M_DT:M_DT + SSD_HEADS] = w[:, OFF_DT:OFF_DT + SSD_HEADS]
            m[:, M_WI:M_WI + HEADS] = w[:, OFF_WI:OFF_WI + HEADS]
            cols.append(m)
        else:
            cols.append(w[:, at:at + P])

    def tiles(blocks):
        return np.ascontiguousarray(np.stack([b.reshape(-1, P, P).transpose(1, 0, 2).reshape(P, -1) for b in blocks]))

    a["w_in"] = tiles(cols)
    a["w_out"] = tiles([w_out[0][:, d * P:(d + 1) * P] for d in range(KT)])
    a["w_gu"] = tiles([m[0][:, j * P:(j + 1) * P] for j in range(FT) for m in (ffn_w_gate, ffn_w_up)])
    rows = FPC * P
    a["w_dn"] = tiles([ffn_w_down[0][c * rows:(c + 1) * rows, d * P:(d + 1) * P] for c in range(FCH) for d in range(KT)])
    pc = np.zeros((P, NPC), f)

    def put(name, v):
        pc[:, PC[name]:PC[name] + v.shape[1]] = v

    def taps(v):
        k = v.shape[0]
        return v.reshape(k, -1, P).transpose(2, 1, 0).reshape(P, -1)

    put("gmix", norm_mix[0].reshape(-1, P).T)
    put("gffn", norm_ffn[0].reshape(-1, P).T)
    put("cw", taps(ssd_conv_w[0]))
    put("cb", ssd_conv_b[0].reshape(-1, P).T)
    put("scw", taps(sc_conv_w[0]))
    put("fcw", taps(ffn_conv_w[0]))
    put("dskip", np.repeat(ssd_d[0], 64).reshape(-1, P).T)
    put("gssd", ssd_norm[0].reshape(-1, P).T)
    put("gq", np.tile(att_q_norm[0], 2)[:, None])
    put("gk", np.tile(att_k_norm[0], 2)[:, None])
    put("dtb", np.tile(ssd_dt_bias[0][None, :], (P, 1)))
    put("alog", np.tile(ssd_a_log[0][None, :], (P, 1)))
    pc[:, PC["eps"]] = EPS
    a["params"] = pc
    a["relb"] = np.ascontiguousarray(rel_bias)
    a["cmats"], a["onehot"] = constants()
    return a


def kernel(**inputs):
    import concourse.bacc as bacc
    from concourse.bass_utils import run_bass_kernel_spmd as run

    f32 = mybir.dt.float32
    nc = bacc.Bacc("TRN2", target_bir_lowering=False, num_devices=1)
    arrays = lay_out(**{k: np.asarray(v) for k, v in inputs.items()})
    args = [nc.dram_tensor(n, v.shape, f32, kind="ExternalInput").ap() for n, v in arrays.items()]
    bias_rows = nc.dram_tensor("bias_rows", (P, HEADS, 384), f32, kind="Internal").ap()
    acs_rows = nc.dram_tensor("acs_rows", (SSD_HEADS, NCH, P), f32, kind="Internal").ap()
    out = nc.dram_tensor("outT", (KT, P, T), f32, kind="ExternalOutput").ap()
    hybrid_block(nc, *args, bias_rows, acs_rows, out)
    got = run(nc, [arrays], core_ids=[0]).results[0]["outT"]
    return np.ascontiguousarray(np.asarray(got).reshape(D, T).T).reshape(1, T, D)
```
